# Optimizing a Trainium2 kernel written in Bass

```python
import math
import jax, jax.numpy as jnp
from jax import lax
import numpy as np

D_MODEL = 2048
BATCH = 1
SEQ = 256
DEPTH = 1

N_HEADS = 8
HEAD_DIM = 128
ATTN_W = N_HEADS * HEAD_DIM
MOBA_BLOCK = 256
MOBA_TOPK = 3
Q_CHUNK = 64
POOL_WINDOWS = (2, 4, 8, 16)
POOL_GROUPS = len(POOL_WINDOWS)
POOL_W = 1024
POOL_GW = POOL_W // POOL_GROUPS
IN_W = 3 * ATTN_W + POOL_W
N_BRANCH = 2
D_FF = 5632
CONV_W = 3
ROPE_THETA = 10000.0
EPS = 1e-6
NEG = -1e30

kernel_name = "hybrid_moba_pool_convffn_block"

def rmsnorm(x, g):
    x32 = x.astype(jnp.float32)
    y = x32 * lax.rsqrt(jnp.mean(x32 * x32, axis=-1, keepdims=True) + EPS)
    return (y * g.astype(jnp.float32)).astype(x.dtype)

def modulate(h, shift, scale):
    return h * (1 + scale[:, None, :]) + shift[:, None, :]

def rope(t, pos):
    half = t.shape[-1] // 2
    inv = ROPE_THETA ** (-jnp.arange(half, dtype=jnp.float32) / half)
    ang = pos.astype(jnp.float32)[:, None] * inv[None, :]
    cos, sin = jnp.cos(ang), jnp.sin(ang)
    t32 = t.astype(jnp.float32)
    t1, t2 = t32[..., :half], t32[..., half:]
    return jnp.concatenate([t1 * cos - t2 * sin, t2 * cos + t1 * sin], axis=-1).astype(t.dtype)

def moba_attention(q, k, v):
    B, H, S, hd = q.shape
    nb = -(-S // MOBA_BLOCK)
    pad = nb * MOBA_BLOCK - S
    k_blk = jnp.pad(k, ((0, 0), (0, 0), (0, pad), (0, 0))).reshape(B, H, nb, MOBA_BLOCK, hd)
    v_blk = jnp.pad(v, ((0, 0), (0, 0), (0, pad), (0, 0))).reshape(B, H, nb, MOBA_BLOCK, hd)
    k_mean = jnp.mean(k_blk.astype(jnp.float32), axis=3)
    topk = min(MOBA_TOPK, nb)
    n_chunks = S // Q_CHUNK
    scale = hd ** -0.5
    b_idx = jnp.arange(B)[:, None, None, None]
    h_idx = jnp.arange(H)[None, :, None, None]
    blk_ids = jnp.arange(nb)

    def one_chunk(ci):
        q0 = ci * Q_CHUNK
        own = q0 // MOBA_BLOCK
        qc = lax.dynamic_slice_in_dim(q, q0, Q_CHUNK, axis=2).astype(jnp.float32) * scale
        qpos = q0 + jnp.arange(Q_CHUNK)
        gate = jnp.einsum('bhqd,bhnd->bhqn', qc, k_mean)
        gate = jnp.where(blk_ids[None, None, None, :] < own, gate, NEG)
        _, sel = lax.top_k(gate, topk)
        valid = sel < own
        k_sel = k_blk[b_idx, h_idx, sel].astype(jnp.float32)
        v_sel = v_blk[b_idx, h_idx, sel].astype(jnp.float32)
        s_sel = jnp.einsum('bhqd,bhqjkd->bhqjk', qc, k_sel)
        s_sel = jnp.where(valid[..., None], s_sel, NEG).reshape(B, H, Q_CHUNK, topk * MOBA_BLOCK)
        k_own = lax.dynamic_index_in_dim(k_blk, own, axis=2, keepdims=False).astype(jnp.float32)
        v_own = lax.dynamic_index_in_dim(v_blk, own, axis=2, keepdims=False).astype(jnp.float32)
        s_own = jnp.einsum('bhqd,bhkd->bhqk', qc, k_own)
        kpos = own * MOBA_BLOCK + jnp.arange(MOBA_BLOCK)
        s_own = jnp.where(kpos[None, :] <= qpos[:, None], s_own, NEG)
        p = jax.nn.softmax(jnp.concatenate([s_sel, s_own], axis=-1), axis=-1)
        p_sel = p[..., :topk * MOBA_BLOCK].reshape(B, H, Q_CHUNK, topk, MOBA_BLOCK)
        p_own = p[..., topk * MOBA_BLOCK:]
        o = (jnp.einsum('bhqjk,bhqjkd->bhqd', p_sel, v_sel)
             + jnp.einsum('bhqk,bhkd->bhqd', p_own, v_own))
        return o.astype(q.dtype)

    out = lax.map(one_chunk, jnp.arange(n_chunks))
    return out.transpose(1, 2, 0, 3, 4).reshape(B, H, S, hd)

def multiscale_pool(u, w_grp, ls):
    B, S, C = u.shape
    u32 = u.astype(jnp.float32)
    cs0 = jnp.concatenate([jnp.zeros((B, 1, C), jnp.float32), jnp.cumsum(u32, axis=1)], axis=1)
    t = jnp.arange(S)
    pooled = []
    for g, w in enumerate(POOL_WINDOWS):
        sl = cs0[..., g * POOL_GW:(g + 1) * POOL_GW]
        lag = jnp.concatenate([jnp.zeros((B, w - 1, POOL_GW), jnp.float32), sl[:, :S - w + 1]], axis=1)
        cnt = jnp.minimum(t + 1, w).astype(jnp.float32)[None, :, None]
        pooled.append((sl[:, 1:] - lag) / cnt)
    d = (jnp.concatenate(pooled, axis=-1) - u32).astype(u.dtype).reshape(B, S, POOL_GROUPS, POOL_GW)
    mixed = jnp.einsum('bsgc,gcd->bsgd', d, w_grp).reshape(B, S, C)
    return mixed * ls

def hybrid_mixer(h, pos, w_in, q_norm_g, k_norm_g, w_pool_grp, pool_scale,
                 w_attn_br, w_pool_br, w_gate, b_gate, w_o):
    B, S, _ = h.shape
    proj = h @ w_in
    q = proj[..., :ATTN_W]
    k = proj[..., ATTN_W:2 * ATTN_W]
    v = proj[..., 2 * ATTN_W:3 * ATTN_W]
    u = proj[..., 3 * ATTN_W:]
    to_heads = lambda t: t.reshape(B, S, N_HEADS, HEAD_DIM).transpose(0, 2, 1, 3)
    q = rope(rmsnorm(to_heads(q), q_norm_g), pos)
    k = rope(rmsnorm(to_heads(k), k_norm_g), pos)
    v = to_heads(v)
    attn = moba_attention(q, k, v).transpose(0, 2, 1, 3).reshape(B, S, ATTN_W)
    y_attn = attn @ w_attn_br
    y_pool = multiscale_pool(u, w_pool_grp, pool_scale) @ w_pool_br
    gates = jax.nn.sigmoid(h @ w_gate + b_gate)
    merged = gates[..., :D_MODEL] * y_attn + gates[..., D_MODEL:] * y_pool
    return merged @ w_o

def conv_glu_ffn(h, w_up, conv_w, conv_b, w_down):
    S = h.shape[1]
    up = h @ w_up
    up_pad = jnp.pad(up, ((0, 0), (CONV_W - 1, 0), (0, 0)))
    conv = conv_b + sum(conv_w[j] * up_pad[:, j:j + S] for j in range(CONV_W))
    a, b = conv[..., :D_FF], conv[..., D_FF:]
    return (jax.nn.silu(a) * b) @ w_down

def setup_inputs(seed: int = 0) -> dict:
    key = jax.random.key(seed)
    ks = jax.random.split(key, 20)
    nrm = lambda k, shape, s: jax.random.normal(k, shape, jnp.float32) * s
    L = DEPTH
    return {
        "x": nrm(ks[0], (BATCH, SEQ, D_MODEL), 1.0),
        "c": nrm(ks[1], (BATCH, D_MODEL), 1.0),
        "w_ada": nrm(ks[2], (L, D_MODEL, 6 * D_MODEL), 0.1 * D_MODEL ** -0.5),
        "b_ada": nrm(ks[3], (L, 6 * D_MODEL), 0.02),
        "norm_mix_g": 1.0 + nrm(ks[4], (L, D_MODEL), 0.02),
        "w_in": nrm(ks[5], (L, D_MODEL, IN_W), D_MODEL ** -0.5),
        "q_norm_g": 1.0 + nrm(ks[6], (L, HEAD_DIM), 0.02),
        "k_norm_g": 1.0 + nrm(ks[7], (L, HEAD_DIM), 0.02),
        "w_pool_grp": nrm(ks[8], (L, POOL_GROUPS, POOL_GW, POOL_GW), POOL_GW ** -0.5),
        "pool_scale": 1.0 + nrm(ks[9], (L, POOL_W), 0.02),
        "w_attn_br": nrm(ks[10], (L, ATTN_W, D_MODEL), ATTN_W ** -0.5),
        "w_pool_br": nrm(ks[11], (L, POOL_W, D_MODEL), POOL_W ** -0.5),
        "w_gate": nrm(ks[12], (L, D_MODEL, N_BRANCH * D_MODEL), D_MODEL ** -0.5),
        "b_gate": nrm(ks[13], (L, N_BRANCH * D_MODEL), 0.02),
        "w_o": nrm(ks[14], (L, D_MODEL, D_MODEL), D_MODEL ** -0.5),
        "norm_ffn_g": 1.0 + nrm(ks[15], (L, D_MODEL), 0.02),
        "w_up": nrm(ks[16], (L, D_MODEL, 2 * D_FF), D_MODEL ** -0.5),
        "conv_w": nrm(ks[17], (L, CONV_W, 2 * D_FF), CONV_W ** -0.5),
        "conv_b": nrm(ks[18], (L, 2 * D_FF), 0.02),
        "w_down": nrm(ks[19], (L, D_FF, D_MODEL), D_FF ** -0.5),
    }

def reference(x, c, w_ada, b_ada, norm_mix_g, w_in, q_norm_g, k_norm_g, w_pool_grp,
              pool_scale, w_attn_br, w_pool_br, w_gate, b_gate, w_o, norm_ffn_g,
              w_up, conv_w, conv_b, w_down):
    S = x.shape[1]
    pos = jnp.arange(S)
    for l in range(DEPTH):
        mod = jax.nn.silu(c) @ w_ada[l] + b_ada[l]
        sh1, sc1, g1, sh2, sc2, g2 = jnp.split(mod, 6, axis=-1)
        h = modulate(rmsnorm(x, norm_mix_g[l]), sh1, sc1)
        x = x + g1[:, None, :] * hybrid_mixer(
            h, pos, w_in[l], q_norm_g[l], k_norm_g[l], w_pool_grp[l], pool_scale[l],
            w_attn_br[l], w_pool_br[l], w_gate[l], b_gate[l], w_o[l])
        h = modulate(rmsnorm(x, norm_ffn_g[l]), sh2, sc2)
        x = x + g2[:, None, :] * conv_glu_ffn(h, w_up[l], conv_w[l], conv_b[l], w_down[l])
    return x


_drawn_inputs = setup_inputs


def setup_inputs(seed=0):
    import zlib

    import numpy as np

    out = dict(_drawn_inputs(seed))
    spreads = {}
    factors = {'b_ada': 3.54,
     'norm_mix_g': 8.0,
     'q_norm_g': 8.0,
     'k_norm_g': 8.0,
     'pool_scale': 28.126,
     'w_attn_br': 7.155,
     'w_gate': 4.617,
     'b_gate': 40.801,
     'norm_ffn_g': 24.214,
     'conv_b': 26.253}
    for name, (base, spread) in spreads.items():
        noise = np.random.default_rng([zlib.crc32(name.encode()), seed]).standard_normal(out[name].shape)
        drawn = base * np.exp(spread * noise) if base else spread * noise
        out[name] = __import__('jax').numpy.asarray(drawn.astype(out[name].dtype))
    for name, factor in factors.items():
        out[name] = (out[name] * factor).astype(out[name].dtype)
    return out
```

```python
from contextlib import ExitStack

import concourse.bass as bass
import numpy as np
from concourse import mybir

F32 = mybir.dt.float32
F32R = mybir.dt.float32r
ALU = mybir.AluOpType
ACT = mybir.ActivationFunctionType
AX = mybir.AxisListType

P = 128
SEQ = 256
D = 2048
DT = D // P
HEADS = 8
HD = 128
POOL_WINDOWS = (2, 4, 8, 16)
PT = 1024 // P
FF = 5632
FT = FF // P
EPS = 1e-6
NEG = -1e30
SCALE = float(HD) ** -0.5
COLS = 512
GT = COLS // P
LOAD_T = 4
CHUNK_T = 2
RAW_SLOTS = 4
CHUNK_SLOTS = 4
PAD = max(POOL_WINDOWS)
QW = P + SEQ

PC_C, PC_GMIX, PC_BADA = 0, 16, 32
PC_GFFN, PC_PSCALE, PC_BGATE, PC_QG, PC_KG = 128, 144, 152, 184, 185
PC_CONV = [256, 384, 512, 640]
FF2T = 2 * FT
PBLOCK_ROWS = [128, 58, FF2T, FF2T, FF2T, FF2T]

ADA_SH1, ADA_SC1, ADA_G1, ADA_SH2, ADA_SC2, ADA_G2 = 0, 4, 8, 12, 16, 20


class Phase:

    def __init__(self, before, bodies, loads, ada):
        self.loads, self.ada = loads, ada
        self.body_loads = 2 * loads + 4 * sum(ada)
        self.body_chunks = 2 * loads * LOAD_T // CHUNK_T
        self.load0 = before.load_end if before else 8 * 4
        self.chunk0 = before.chunk_end if before else 0
        self.group0 = before.group_end if before else 0
        self.ada0 = before.ada_end if before else 8
        self.load_end = self.load0 + bodies * self.body_loads
        self.chunk_end = self.chunk0 + bodies * self.body_chunks
        self.group_end = self.group0 + bodies * 2
        self.ada_end = self.ada0 + bodies * sum(ada)

    def group(self, it, g):
        return it * 2 + (self.group0 + g)

    def chunk(self, it, g, c):
        return it * self.body_chunks + (self.chunk0 + g * (self.body_chunks // 2) + c)

    def chunk_slot(self, g, c):
        return (g * (self.body_chunks // 2) + c) % CHUNK_SLOTS

    def order(self, g):
        seq = [("main", m) for m in range(self.loads)]
        if self.ada[g]:
            seq = seq[:2] + [("ada", 0), ("ada", 1)] + seq[2:3] + [("ada", 2), ("ada", 3)] + seq[3:]
        return seq

    def pos(self, g, kind, n):
        return (self.loads + 4 * self.ada[0]) * g + self.order(g).index((kind, n))

    def load(self, it, pos):
        return it * self.body_loads + (self.load0 + pos)

    def slot(self, it, pos):
        if isinstance(it, int):
            return self.load(it, pos) % RAW_SLOTS
        assert self.load0 % RAW_SLOTS == 0 and self.body_loads % RAW_SLOTS == 0
        return pos % RAW_SLOTS

    def landed(self, it, pos):
        if isinstance(it, int):
            return 16 * (self.load(it, pos) // RAW_SLOTS + 1)
        return it * (16 * self.body_loads // RAW_SLOTS) + 16 * ((self.load0 + pos) // RAW_SLOTS + 1)

    def used(self, it, pos, half):
        return it * (2 * self.body_loads) + (2 * (self.load0 + pos) + half)


PH_U = Phase(None, 1, 4, (1, 0))
PH_QK = Phase(PH_U, 2, 4, (1, 0))
PH_V = Phase(PH_QK, 1, 4, (1, 0))
PH_GATE = Phase(PH_V, 4, 4, (1, 0))
PH_BR = Phase(PH_GATE, 4, 2, (0, 0))
PH_WO = Phase(PH_BR, 2, 4, (1, 1))
PH_UP = Phase(PH_WO, 11, 4, (0, 0))
PH_DOWN = Phase(PH_UP, 2, 11, (1, 1))


class Tally:

    def __init__(self, sem):
        self.sem, self.n, self.extra = sem, 0, None

    def inc(self, instruction):
        instruction.then_inc(self.sem, 1)
        self.n += 1

    def value(self):
        return self.n if self.extra is None else self.extra + self.n

    def enter(self, it, per, first=0):
        self.start, self.per = self.n, per
        self.extra = it * per + (-first * per)

    def leave(self, count):
        assert self.n - self.start == self.per, (self.n - self.start, self.per)
        self.n = self.start + count * self.per
        self.extra = None


def build_block(nc, x, c, w_ada, b_ada, norm_mix_g, w_in, q_norm_g, k_norm_g, w_pool_grp,
                pool_scale, w_attn_br, w_pool_br, w_gate, b_gate, w_o, norm_ffn_g, w_up,
                conv_w, conv_b, w_down, k_square, k_rope, k_mask, k_invcnt, out, x1_spill):
    ctx = ExitStack()
    with ctx:
        cursor = [nc.sbuf_base + (-nc.sbuf_base) % 64]

        def at(name, shape, dt, offset):
            return nc.alloc_sbuf_tensor_at(name, shape, dt, offset=offset)

        def keep(name, shape, dt=F32):
            t = at(name, shape, dt, cursor[0])
            cursor[0] += int(np.prod(shape[1:])) * 4
            cursor[0] += (-cursor[0]) % 32
            return t

        def sem(name):
            return ctx.enter_context(nc.semaphore(name))

        raw = keep("raw", [P, RAW_SLOTS, LOAD_T, COLS])
        w_hi = keep("w_hi", [P, CHUNK_SLOTS, CHUNK_T, COLS], F32R)
        w_lo = keep("w_lo", [P, CHUNK_SLOTS, CHUNK_T, COLS], F32R)
        square = keep("square", [P, 2, P])
        par = keep("par", [P, 6 * P])
        mod = keep("mod", [P, 6 * DT])
        silu_c = keep("silu_c", [P, DT])
        scale_a = keep("scale_a", [P, DT])
        eps = keep("eps", [P, 1])
        ada_acc = keep("ada_acc", [P, COLS])
        h0 = cursor[0]
        hT = keep("hT", [P, DT, 2 * SEQ], F32R)
        x0 = cursor[0]
        xT = keep("xT", [P, DT, SEQ])
        cursor[0] += 64
        big = cursor[0]
        actT = keep("actT", [P, FT, 2 * SEQ], F32R)
        ident, ones = square[:, 0, :], square[:, 1, :]

        attnT = at("attnT", [P, HEADS, 2 * SEQ], F32R, big)
        poolT = at("poolT", [P, PT, 2 * SEQ], F32R, big + 16384)
        qk = at("qk", [P, 2 * HEADS, SEQ], F32, big + 32768)
        v_tok = at("v_tok", [P, 2, HEADS * HD], F32, big + 49152)
        u_pad = at("u_pad", [P, PT, PAD + SEQ], F32, big + 57344)
        w_pool = at("w_pool", [P, 4, 2, 256], F32, big + 66048)
        gates = at("gates", [P, 2 * DT, SEQ], F32, big + 32768)
        y_attn = at("y_attn", [P, GT, SEQ], F32, big + 66048)
        y_sum = at("y_sum", [P, GT, SEQ], F32, big + 70144)
        rope_c = at("rope_c", [P, 2 * SEQ + P], F32, big + 74240)
        mask = at("mask", [P, QW], F32, big + 76800)
        invcnt = at("invcnt", [P, 4, SEQ], F32, big + 78336)
        half_a = at("half_a", [P, GT, SEQ], F32, big + 82432)
        assert big + 82432 + 4096 <= big + FT * 2 * SEQ * 4
        x_tok = at("x_tok", [P, 2, D], F32, big)
        par_rows = at("par_rows", [P, 6, P], F32, big + 16384)
        sq_x = at("sq_x", [P, 2, 2 * SEQ], F32, big + 20480)
        ss_x = at("ss_x", [P, SEQ], F32, big + 86528)
        rs_x = at("rs_x", [P, SEQ], F32, big + 87552)
        t_x = at("t_x", [P, 2, SEQ], F32, big + 26624)
        pool_s = [at(f"pool_s{n}", [P, PT, PAD + SEQ], F32, big + n * 8704) for n in range(2)]
        tg = at("tg", [P, 4, SEQ], F32, big + 17408)
        sq = at("sq", [P, 4, SEQ], F32, big + 21504)
        rt = at("rt", [P, 2, SEQ], F32, big + 25600)
        ra = at("ra", [P, SEQ], F32, big + 27648)
        rb = at("rb", [P, SEQ], F32, big + 28672)
        rr = at("rr", [P, SEQ], F32, big + 29696)
        probs = at("probs", [P, 2, QW], F32, big + 17408)
        probsT = at("probsT", [P, 2, QW], F32, big + 20480)
        stat = at("stat", [P, 2, 8], F32, big + 23552)
        sq_x1 = at("sq_x1", [P, GT, SEQ], F32, big)
        t_x1 = at("t_x1", [P, 2, SEQ], F32, big + 4096)
        half_b = at("half_b", [P, GT, SEQ], F32, x0)
        up_pad = at("up_pad", [P, GT, 2 + SEQ], F32, x0 + 4096)
        conv_a = at("conv_a", [P, GT, SEQ], F32, x0 + 4096 + 4128)
        conv_b_ = at("conv_bb", [P, GT, SEQ], F32, x0 + 8192 + 4128)
        x2T = at("x2T", [P, DT, SEQ], F32, h0)
        out_tok = at("out_tok", [P, 4, 2, COLS], F32, h0 + 16384)

        bank = [ctx.enter_context(nc.psum_tensor(f"bank{n}", [P, 512], F32)) for n in range(8)]

        x_in, par_in, square_in, const_in = sem("x_in"), sem("par_in"), sem("square_in"), sem("const_in")
        wp_in = sem("wp_in")
        raw_full = [sem(f"raw_full{n}") for n in range(RAW_SLOTS)]
        half_used = sem("half_used")
        hi_ready = sem("hi_ready")
        chunk_used = sem("chunk_used")
        half_ready = sem("half_ready")
        sum_ready = sem("sum_ready")
        ada_sum = sem("ada_sum")
        mod_ready = sem("mod_ready")
        dve_step = sem("dve_step")
        act_step = sem("act_step")
        pool_step = sem("pool_step")
        xt_mm, xt_ready = sem("xt_mm"), sem("xt_ready")
        par_mm, par_ready = sem("par_mm"), sem("par_ready")
        silu_ready = sem("silu_ready")
        eps_ready = sem("eps_ready")
        sqx_ready, sqx_used = sem("sqx_ready"), sem("sqx_used")
        ss_ready, ss_mm, rt_ready, rs_ready = sem("ss_ready"), sem("ss_mm"), sem("rt_ready"), sem("rs_ready")
        t_ready, h_hi, h_ready = sem("t_ready"), sem("h_hi"), sem("h_ready")
        d_ready = sem("d_ready")
        rope_in, rope_mm, rope_rt, rope_out = sem("rope_in"), sem("rope_mm"), sem("rope_rt"), sem("rope_out")
        s_mm, max_ready, exp_ready, probs_ready = sem("s_mm"), sem("max_ready"), sem("exp_ready"), sem("probs_ready")
        pt_mm, pt_ready, o_mm, o_hi, attn_ready = sem("pt_mm"), sem("pt_ready"), sem("o_mm"), sem("o_hi"), sem("attn_ready")
        mix_mm, mix_hi, pool_ready = sem("mix_mm"), sem("mix_hi"), sem("pool_ready")
        gate_ready = sem("gate_ready")
        merge_sum, merge_hi, merged_ready = sem("merge_sum"), sem("merge_hi"), sem("merged_ready")
        x1_ready, sq1_ready = sem("x1_ready"), sem("sq1_ready")
        tap2_ready, taps_ready, silu_a = sem("tap2_ready"), sem("taps_ready"), sem("silu_a")
        glu_ready, act_hi, act_ready = sem("glu_ready"), sem("act_hi"), sem("act_ready")
        spilled, x1_back = sem("spilled"), sem("x1_back")
        x2_ready, out_mm, out_copied, stored = sem("x2_ready"), sem("out_mm"), sem("out_copied"), sem("stored")

        def tiles(w):
            return w.rearrange("(t p) n -> p t n", p=P)

        def rows(w, t0, col):
            return tiles(w)[:, t0:t0 + LOAD_T, bass.ds(col, COLS)]

        def flat(w):
            return w.rearrange("(t p) -> t p", p=P)

        block = ctx.enter_context(nc.Block())

        @block.sync
        def _(sp):
            def load(src, it, ph, pos):
                slot = ph.slot(it, pos)
                sp.wait_ge(half_used, ph.used(it, pos - RAW_SLOTS, 2))
                sp.dma_start(raw[:, slot, :, :], src).then_inc(raw_full[slot], 16)

            def body(ph, it, mains, adas):
                pos = 0
                for g in range(2):
                    for kind, n in ph.order(g):
                        w, col, a = (*mains[g], 0) if kind == "main" else (w_ada[0], adas[g] * COLS, 1)
                        load(rows(w, n * LOAD_T, col), it, ph, pos)
                        pos += 1

            sp.dma_start(x_tok[:, :, :], x[0].rearrange("(t p) n -> p t n", p=P)).then_inc(x_in, 16)
            sp.dma_start(square[:, :, :], k_square).then_inc(square_in, 16)
            for r0, blk, src in ((0, 0, flat(c[0])), (16, 0, flat(norm_mix_g[0])), (32, 0, flat(b_ada[0])),
                                 (0, 1, flat(norm_ffn_g[0])), (16, 1, flat(pool_scale[0])),
                                 (24, 1, flat(b_gate[0])), (56, 1, q_norm_g), (57, 1, k_norm_g),
                                 (0, 2, flat(conv_w[0, 0])), (0, 3, flat(conv_w[0, 1])),
                                 (0, 4, flat(conv_w[0, 2])), (0, 5, flat(conv_b[0]))):
                sp.dma_start(par_rows[r0:r0 + src.shape[0], blk, :], src).then_inc(par_in, 16)
            for q in range(RAW_SLOTS):
                sp.dma_start(raw[:, q, :, :], rows(w_ada[0], q * LOAD_T, 0)).then_inc(raw_full[q], 16)
            with sp.Fori(1, 8) as it:
                for q in range(RAW_SLOTS):
                    sp.wait_ge(half_used, it * (2 * RAW_SLOTS) + 2 * (q - RAW_SLOTS + 1))
                    sp.dma_start(raw[:, q, :, :], rows(w_ada[0], q * LOAD_T, it * COLS)).then_inc(raw_full[q], 16)
            sp.dma_start(rope_c[:, :], k_rope).then_inc(const_in, 16)
            sp.dma_start(mask[:, :], k_mask).then_inc(const_in, 16)
            sp.dma_start(invcnt[:, :, :], k_invcnt).then_inc(const_in, 16)
            sp.dma_start(w_pool[:, :, :, :].rearrange("p g t n -> p (g t) n"),
                         w_pool_grp[0].rearrange("g (t p) n -> p (g t) n", p=P)).then_inc(wp_in, 16)
            body(PH_U, 0, [(w_in[0], 3072), (w_in[0], 3584)], [ADA_SC2, 0])
            with sp.Fori(0, 2) as it:
                body(PH_QK, it, [(w_in[0], it * COLS), (w_in[0], it * COLS + 1024)], [it + (ADA_SC2 + 1), 0])
            body(PH_V, 0, [(w_in[0], 2048), (w_in[0], 2560)], [ADA_SC2 + 3, 0])
            with sp.Fori(0, 4) as it:
                body(PH_GATE, it, [(w_gate[0], it * COLS), (w_gate[0], it * COLS + D)], [it + ADA_SH2, 0])
            with sp.Fori(0, 4) as it:
                body(PH_BR, it, [(w_attn_br[0], it * COLS), (w_pool_br[0], it * COLS)], [0, 0])
            with sp.Fori(0, 2) as it:
                body(PH_WO, it, [(w_o[0], it * (2 * COLS)), (w_o[0], it * (2 * COLS) + COLS)],
                     [it * 2 + ADA_G1, it * 2 + (ADA_G1 + 1)])
            with sp.Fori(0, 11) as it:
                body(PH_UP, it, [(w_up[0], it * COLS), (w_up[0], it * COLS + FF)], [0, 0])
            for it in range(2):
                body(PH_DOWN, it, [(w_down[0], 2 * it * COLS), (w_down[0], (2 * it + 1) * COLS)],
                     [ADA_G2 + 2 * it, ADA_G2 + 2 * it + 1])

        @block.gpsimd
        def _(pool):
            step = Tally(pool_step)

            def link(ins):
                step.inc(ins)
                pool.wait_ge(pool_step, step.value())

            nc.gpsimd.memset(eps[:, :], EPS).then_inc(eps_ready, 1)
            pool.wait_ge(xt_mm, 8)
            pool.wait_ge(par_mm, 2)
            for t in (u_pad, pool_s[0], pool_s[1]):
                link(nc.gpsimd.memset(t[:, :, 0:PAD], 0.0))
            pool.wait_ge(sum_ready, 2 * GT)
            pool.wait_ge(const_in, 48)
            src = u_pad
            for n, w in enumerate(POOL_WINDOWS):
                dst, other, t0 = pool_s[n % 2], pool_s[(n + 1) % 2], 2 * n
                link(nc.gpsimd.tensor_tensor(dst[:, t0:, PAD:], src[:, t0:, PAD:],
                                             src[:, t0:, PAD - w // 2:PAD + SEQ - w // 2], ALU.add))
                for t in (t0, t0 + 1):
                    link(nc.gpsimd.tensor_tensor(other[:, t, PAD:], dst[:, t, PAD:], invcnt[:, n, :], ALU.mult))
                    last = nc.gpsimd.tensor_tensor(u_pad[:, t, PAD:], other[:, t, PAD:], u_pad[:, t, PAD:], ALU.subtract)
                    if n < len(POOL_WINDOWS) - 1 or t == t0:
                        link(last)
                src = dst
            last.then_inc(d_ready, 1)

        @block.scalar
        def _(act):
            act_tally = Tally(act_step)

            def hi_chunk(ph, it, g, c):
                pos = ph.pos(g, "main", c * CHUNK_T // LOAD_T)
                if not (ph is PH_U and g == 0 and c < CHUNK_SLOTS):
                    act.wait_ge(chunk_used, ph.chunk(it, g, c - CHUNK_SLOTS + 1))
                if c % 2 == 0:
                    act.wait_ge(raw_full[ph.slot(it, pos)], ph.landed(it, pos))
                t0 = (c % 2) * CHUNK_T
                nc.scalar.activation(w_hi[:, ph.chunk_slot(g, c), :, :], raw[:, ph.slot(it, pos), t0:t0 + CHUNK_T, :],
                                     ACT.Copy).then_inc(hi_ready, 1)

            def head(ph, it, g):
                for c in range(4):
                    hi_chunk(ph, it, g, c)

            def rest(ph, it, g):
                for c in range(4, ph.loads * 2):
                    hi_chunk(ph, it, g, c)

            def halves(ph, it, g, half):
                G = ph.group(it, g)
                act.wait_ge(chunk_used, ph.chunk(it, g, ph.body_chunks // 2))
                if not (ph is PH_U and g == 0):
                    act.wait_ge(sum_ready, G * GT)
                for ft in range(GT):
                    b = bank[4 * (g % 2) + ft]
                    nc.scalar.activation(half[:, ft, :], b[:, SEQ:2 * SEQ], ACT.Copy).then_inc(half_ready, 1)

            act.wait_ge(par_mm, 1)
            nc.scalar.activation(par[:, 0:P], bank[7][:, 0:P], ACT.Copy).then_inc(par_ready, 1)
            act.wait_ge(par_ready, 1)
            nc.scalar.activation(silu_c[:, :], par[:, PC_C:PC_C + DT], ACT.Silu).then_inc(silu_ready, 1)
            for b in range(8):
                act.wait_ge(xt_mm, b + 1)
                nc.scalar.activation(xT[:, 2 * b:2 * b + 2, :].rearrange("p t n -> p (t n)"), bank[b][:, :],
                                     ACT.Copy).then_inc(xt_ready, 1)
                act.wait_ge(xt_ready, b + 1)
                if b >= 2:
                    act.wait_ge(sqx_used, b - 1)
                nc.scalar.activation(sq_x[:, b % 2, :], xT[:, 2 * b:2 * b + 2, :].rearrange("p t n -> p (t n)"),
                                     ACT.Square).then_inc(sqx_ready, 1)
            act.wait_ge(par_mm, 2)
            for n in range(1, 6):
                r = PBLOCK_ROWS[n]
                b, o = (bank[5], (n - 1) * P) if n < 5 else (bank[6], 0)
                last = nc.scalar.activation(par[:, n * P:n * P + r], b[:, o:o + r], ACT.Copy)
            last.then_inc(par_ready, 1)
            act.wait_ge(ss_mm, 1)
            act.wait_ge(eps_ready, 1)
            nc.scalar.activation(rs_x[:, :], bank[4][:, 0:SEQ], ACT.Sqrt, bias=eps[:, 0:1], scale=1.0 / D).then_inc(rt_ready, 1)

            def norm_hi(first, shift, buf):
                for t in range(DT):
                    act.wait_ge(t_ready, first + t + 1)
                    nc.scalar.activation(hT[:, t, 0:SEQ], buf[:, t % 2, :], ACT.Identity,
                                         bias=mod[:, shift + t:shift + t + 1]).then_inc(h_hi, 1)

            norm_hi(0, ADA_SH1 * GT, t_x)

            head(PH_U, 0, 0)
            rest(PH_U, 0, 0)
            head(PH_U, 0, 1)
            halves(PH_U, 0, 0, half_a)
            rest(PH_U, 0, 1)
            head(PH_QK, 0, 0)
            halves(PH_U, 0, 1, half_a)
            with act.Fori(0, 2) as it:
                rest(PH_QK, it, 0)
                head(PH_QK, it, 1)
                halves(PH_QK, it, 0, half_a)
                rest(PH_QK, it, 1)
                head(PH_QK, it + 1, 0)
                halves(PH_QK, it, 1, half_a)

            def v_half(g):
                act.wait_ge(chunk_used, PH_V.chunk(0, g, PH_V.body_chunks // 2))
                nc.scalar.activation(v_tok[:, 0, g * COLS:(g + 1) * COLS], bank[4 * g][:, :], ACT.Copy).then_inc(half_ready, GT)

            rest(PH_V, 0, 0)
            head(PH_V, 0, 1)
            v_half(0)
            rest(PH_V, 0, 1)
            head(PH_GATE, 0, 0)
            v_half(1)

            def rope_root(i):
                act.wait_ge(rope_mm, i + 1)
                if i >= 2:
                    act.wait_ge(rope_out, i - 1)
                nc.scalar.activation(rt[:, i % 2, :], bank[i % 8][:, SEQ:2 * SEQ], ACT.Sqrt, bias=eps[:, 0:1],
                                     scale=1.0 / HD).then_inc(rope_rt, 1)

            act.wait_ge(d_ready, 1)
            act.wait_ge(sum_ready, PH_QK.group_end * GT)
            for i in range(2 * HEADS):
                if i >= 4:
                    act.wait_ge(rope_out, i - 3)
                gain = par[:, PC_QG:PC_QG + 1] if i < HEADS else par[:, PC_KG:PC_KG + 1]
                nc.scalar.activation(tg[:, i % 4, :], qk[:, i, :], ACT.Copy, scale=gain).then_inc(rope_in, 1)
                nc.scalar.activation(sq[:, i % 4, :], qk[:, i, :], ACT.Square).then_inc(rope_in, 1)
                if i >= 2:
                    rope_root(i - 2)
            rope_root(2 * HEADS - 2)
            rope_root(2 * HEADS - 1)

            for i in range(HEADS + 2):
                if i < HEADS:
                    act.wait_ge(max_ready, i + 1)
                    nc.scalar.activation(probs[:, i % 2, 0:P], probs[:, i % 2, 0:P], ACT.Exp, bias=stat[:, i % 2, 2:3],
                                         scale=SCALE, accum_out=stat[:, i % 2, 4:5])
                    nc.scalar.activation(probs[:, i % 2, P:QW], probs[:, i % 2, P:QW], ACT.Exp, bias=stat[:, i % 2, 3:4],
                                         scale=SCALE, accum_out=stat[:, i % 2, 5:6]).then_inc(exp_ready, 1)
                h = i - 1
                if 0 <= h < HEADS:
                    act.wait_ge(pt_mm, h + 1)
                    if h >= 2:
                        act.wait_ge(o_mm, h - 1)
                    nc.scalar.activation(probsT[:, h % 2, :], bank[2 + h % 2][:, 0:QW], ACT.Copy).then_inc(pt_ready, 1)
                h = i - 2
                if h >= 0:
                    act.wait_ge(o_mm, h + 1)
                    nc.scalar.activation(attnT[:, h, 0:SEQ], bank[4 + h % 2][:, 0:SEQ], ACT.Copy).then_inc(o_hi, 1)
            for o in range(PT):
                act.wait_ge(mix_mm, o + 1)
                if o == 0:
                    act.wait_ge(o_mm, HEADS)
                    act.wait_ge(probs_ready, HEADS)
                nc.scalar.activation(poolT[:, o, 0:SEQ], bank[6 + o % 2][:, 0:SEQ], ACT.Copy,
                                     scale=par[:, PC_PSCALE + o:PC_PSCALE + o + 1]).then_inc(mix_hi, 1)

            def sigmoids(it, g):
                for ft in range(GT):
                    act.wait_ge(sum_ready, it * (2 * GT) + ((PH_GATE.group0 + g) * GT + ft + 1))
                    t = it * GT + (g * DT + ft)
                    nc.scalar.activation(gates[:, bass.ds(t, 1), :], gates[:, bass.ds(t, 1), :], ACT.Sigmoid,
                                         bias=par[:, bass.ds(t + PC_BGATE, 1)]).then_inc(gate_ready, 1)

            with act.Fori(0, 4) as it:
                rest(PH_GATE, it, 0)
                head(PH_GATE, it, 1)
                halves(PH_GATE, it, 0, half_a)
                sigmoids(it, 0)
                rest(PH_GATE, it, 1)
                head(PH_GATE, it + 1, 0)
                halves(PH_GATE, it, 1, half_a)
                sigmoids(it, 1)
            with act.Fori(0, 4) as it:
                head(PH_BR, it, 1)
                halves(PH_BR, it, 0, half_a)
                head(PH_BR, it + 1, 0)
                halves(PH_BR, it, 1, half_a)
                for ft in range(GT):
                    act.wait_ge(merge_sum, it * GT + (ft + 1))
                    nc.scalar.activation(hT[:, bass.ds(it * GT + ft, 1), 0:SEQ], y_sum[:, ft:ft + 1, :],
                                         ACT.Copy).then_inc(merge_hi, 1)
            with act.Fori(0, 2) as it:
                for g in range(2):
                    rest(PH_WO, it, g)
                    head(PH_WO, it + g, 1 - g)
                    halves(PH_WO, it, g, half_a)
                    for ft in range(GT):
                        act.wait_ge(x1_ready, it * (2 * GT) + (g * GT + ft + 1))
                        nc.scalar.activation(sq_x1[:, ft:ft + 1, :], xT[:, bass.ds(it * (2 * GT) + (g * GT + ft), 1), :],
                                             ACT.Square).then_inc(sq1_ready, 1)
            act.dma_start(x1_spill.rearrange("p (t n) -> p t n", n=SEQ), xT[:, :, :]).then_inc(spilled, 16)
            act.wait_ge(ss_mm, 2)
            nc.scalar.activation(rs_x[:, :], bank[0][:, 0:SEQ], ACT.Sqrt, bias=eps[:, 0:1], scale=1.0 / D).then_inc(rt_ready, 1)
            norm_hi(DT, ADA_SH2 * GT, t_x1)
            act.wait_ge(spilled, 16)

            def tap2(it, g):
                for ft in range(GT):
                    act.wait_ge(sum_ready, it * (2 * GT) + ((PH_UP.group0 + g) * GT + ft + 1))
                    t = it * GT + (g * FT + ft)
                    dst = conv_a if g == 0 else conv_b_
                    nc.scalar.activation(dst[:, ft:ft + 1, :], up_pad[:, ft:ft + 1, 2:], ACT.Identity,
                                         bias=par[:, bass.ds(t + PC_CONV[3], 1)],
                                         scale=par[:, bass.ds(t + PC_CONV[2], 1)]).then_inc(tap2_ready, 1)

            with act.Fori(0, 11) as it:
                rest(PH_UP, it, 0)
                head(PH_UP, it, 1)
                halves(PH_UP, it, 0, half_b)
                tap2(it, 0)
                for ft in range(GT):
                    act.wait_ge(taps_ready, it * (2 * GT) + (ft + 1))
                    nc.scalar.activation(conv_a[:, ft, :], conv_a[:, ft, :], ACT.Silu).then_inc(silu_a, 1)
                rest(PH_UP, it, 1)
                head(PH_UP, it + 1, 0)
                halves(PH_UP, it, 1, half_b)
                tap2(it, 1)
                for ft in range(GT):
                    act.wait_ge(glu_ready, it * GT + (ft + 1))
                    nc.scalar.activation(actT[:, bass.ds(it * GT + ft, 1), 0:SEQ], conv_b_[:, ft:ft + 1, :],
                                         ACT.Copy).then_inc(act_hi, 1)
            act.wait_ge(chunk_used, PH_UP.chunk_end)
            act.dma_start(x2T[:, :, :], x1_spill.rearrange("p (t n) -> p t n", n=SEQ)).then_inc(x1_back, 16)
            for it in range(2):
                for g in range(2):
                    rest(PH_DOWN, it, g)
                    if it + g < 2:
                        head(PH_DOWN, it + g, 1 - g)
                    halves(PH_DOWN, it, g, half_b)
            for G in range(4):
                act.wait_ge(out_mm, G + 1)
                nc.scalar.activation(out_tok[:, G, 0, :], bank[2 * G][:, :], ACT.Copy).then_inc(act_step, 1)
                act.wait_ge(act_step, G + 1)
                act.dma_start(out[0, 0:P, G * COLS:(G + 1) * COLS], out_tok[:, G, 0, :]).then_inc(stored, 16)
            for G in range(4):
                act.wait_ge(out_copied, G + 1)
                act.dma_start(out[0, P:2 * P, G * COLS:(G + 1) * COLS], out_tok[:, G, 1, :]).then_inc(stored, 16)
            act.wait_ge(stored, 8 * 16)

        @block.vector
        def _(dve):
            step = Tally(dve_step)

            def link(ins):
                step.inc(ins)
                dve.wait_ge(dve_step, step.value())

            def lo_chunk(ph, it, g, c):
                pos = ph.pos(g, "main", c * CHUNK_T // LOAD_T)
                t0, sc = (c % 2) * CHUNK_T, ph.chunk_slot(g, c)
                dve.wait_ge(hi_ready, ph.chunk(it, g, c) + 1)
                nc.vector.tensor_tensor(w_lo[:, sc, :, :], raw[:, ph.slot(it, pos), t0:t0 + CHUNK_T, :],
                                        w_hi[:, sc, :, :].bitcast(F32), ALU.subtract).then_inc(half_used, 1)

            def ada_load(q, slot, landed, sums):
                dve.wait_ge(raw_full[slot], landed)
                if q == 0 and sums is not None:
                    dve.wait_ge(ada_sum, sums)
                for t in range(LOAD_T):
                    k = q * LOAD_T + t
                    w, s = raw[:, slot, t, :], silu_c[:, k:k + 1]
                    if k == 0:
                        ins = nc.vector.tensor_scalar(ada_acc[:, :], w, s, None, ALU.mult)
                    else:
                        ins = nc.vector.scalar_tensor_tensor(out=ada_acc[:, :], in0=w, scalar=s, in1=ada_acc[:, :],
                                                             op0=ALU.mult, op1=ALU.add)
                    if t < LOAD_T - 1:
                        link(ins)
                    else:
                        ins.then_inc(half_used, 2)

            def mod_store(sums, w, b):
                dve.wait_ge(ada_sum, sums)
                nc.vector.tensor_tensor(mod[:, bass.ds(w * GT, GT)], bank[b][:, 0:GT],
                                        par[:, bass.ds(w * GT + PC_BADA, GT)], ALU.add).then_inc(mod_ready, 1)

            def head(ph, it, g, ada=None):
                for c in range(4):
                    lo_chunk(ph, it, g, c)
                    if c == 2 and ada:
                        mod_store(*ada)

            def rest(ph, it, g):
                for kind, n in ph.order(g)[2:]:
                    pos = ph.pos(g, kind, n)
                    if kind == "main":
                        lo_chunk(ph, it, g, 2 * n)
                        lo_chunk(ph, it, g, 2 * n + 1)
                    else:
                        if n:
                            dve.wait_ge(half_used, ph.used(it, pos, 0))
                        ada_load(n, ph.slot(it, pos), ph.landed(it, pos),
                                 it * sum(ph.ada) + (ph.ada0 + ph.ada[0] * g))

            def sums(ph, it, g, dst, half, then=None):
                for ft in range(GT):
                    dve.wait_ge(half_ready, it * (2 * GT) + ((ph.group0 + g) * GT + ft + 1))
                    nc.vector.tensor_tensor(dst(ft), bank[4 * g + ft][:, 0:SEQ], half[:, ft, :], ALU.add).then_inc(sum_ready, 1)
                    if then:
                        dve.wait_ge(sum_ready, it * (2 * GT) + ((ph.group0 + g) * GT + ft + 1))
                        then(ft)

            def norm(first, gain, scale, buf):
                dve.wait_ge(rt_ready, 1 if first == 0 else 2)
                link(nc.vector.reciprocal(rs_x[:, :], rs_x[:, :]))
                link(nc.vector.scalar_tensor_tensor(out=scale_a[:, :], in0=mod[:, scale:scale + DT], scalar=1.0,
                                                    in1=par[:, gain:gain + DT], op0=ALU.add, op1=ALU.mult))

                def lo(t):
                    shift = (ADA_SH1 if first == 0 else ADA_SH2) * GT + t
                    dve.wait_ge(h_hi, first + t + 1)
                    nc.vector.scalar_tensor_tensor(out=hT[:, t, SEQ:], in0=buf[:, t % 2, :], scalar=mod[:, shift:shift + 1],
                                                   in1=hT[:, t, 0:SEQ].bitcast(F32), op0=ALU.add,
                                                   op1=ALU.subtract).then_inc(h_ready, 1)

                for t in range(DT):
                    if t >= 2:
                        dve.wait_ge(h_ready, first + t - 1)
                    nc.vector.scalar_tensor_tensor(out=buf[:, t % 2, :], in0=xT[:, t, :], scalar=scale_a[:, t:t + 1],
                                                   in1=rs_x[:, :], op0=ALU.mult, op1=ALU.mult).then_inc(t_ready, 1)
                    if t >= 1:
                        lo(t - 1)
                lo(DT - 1)

            for b in range(8):
                dve.wait_ge(sqx_ready, b + 1)
                sq2 = sq_x[:, b % 2, :]
                if b == 0:
                    nc.vector.tensor_tensor(ss_x[:, :], sq2[:, 0:SEQ], sq2[:, SEQ:], ALU.add).then_inc(sqx_used, 1)
                else:
                    dve.wait_ge(sqx_used, b)
                    link(nc.vector.tensor_tensor(ss_x[:, :], ss_x[:, :], sq2[:, 0:SEQ], ALU.add))
                    nc.vector.tensor_tensor(ss_x[:, :], ss_x[:, :], sq2[:, SEQ:], ALU.add).then_inc(sqx_used, 1)
            dve.wait_ge(silu_ready, 1)
            dve.wait_ge(par_ready, 2)

            def ada_group(it, first):
                for q in range(LOAD_T):
                    if not (first and q == 0):
                        dve.wait_ge(half_used, it * 8 + 2 * q)
                    ada_load(q, q, it * 16 + 16, None if first else it)
                mod_store(it + 1, it, 0)

            ada_group(0, True)
            with dve.Fori(1, 8) as it:
                step.enter(it, 12, 1)
                ada_group(it, False)
                step.leave(7)
            dve.wait_ge(mod_ready, 8)
            norm(0, PC_GMIX, ADA_SC1 * GT, t_x)

            head(PH_U, 0, 0)
            for g in range(2):
                rest(PH_U, 0, g)
                head(PH_U if g == 0 else PH_QK, 0, 1 - g, (PH_U.ada0 + 1, ADA_SC2, 4) if g == 0 else None)
                sums(PH_U, 0, g, lambda ft: u_pad[:, g * GT + ft, PAD:], half_a)
            with dve.Fori(0, 2) as it:
                step.enter(it, 12)
                for g in range(2):
                    rest(PH_QK, it, g)
                    head(PH_QK, it + g, 1 - g, (it + PH_QK.ada0 + 1, it + (ADA_SC2 + 1), 4) if g == 0 else None)
                    sums(PH_QK, it, g, lambda ft: qk[:, bass.ds(it * GT + (HEADS * g + ft), 1), :].rearrange("p a n -> p (a n)"), half_a)
                step.leave(2)
            for g in range(2):
                rest(PH_V, 0, g)
                head(PH_V if g == 0 else PH_GATE, 0, 1 - g, (PH_V.ada0 + 1, ADA_SC2 + 3, 4) if g == 0 else None)
                dve.wait_ge(half_ready, (PH_V.group0 + g + 1) * GT)
                nc.vector.tensor_copy(v_tok[:, 1, g * COLS:(g + 1) * COLS], bank[4 * g + 1][:, :]).then_inc(sum_ready, GT)

            dve.wait_ge(d_ready, 1)
            for i in range(2 * HEADS):
                dve.wait_ge(rope_rt, i + 1)
                link(nc.vector.tensor_tensor(ra[:, :], tg[:, i % 4, :], rope_c[:, 0:SEQ], ALU.mult))
                link(nc.vector.tensor_tensor(rb[:, :], bank[i % 8][:, 0:SEQ], rope_c[:, SEQ:2 * SEQ], ALU.mult))
                link(nc.vector.tensor_tensor(ra[:, :], ra[:, :], rb[:, :], ALU.add))
                link(nc.vector.reciprocal(rr[:, :], rt[:, i % 2, :]))
                nc.vector.tensor_tensor(qk[:, i, :], ra[:, :], rr[:, :], ALU.mult).then_inc(rope_out, 1)
                dve.wait_ge(rope_out, i + 1)
            for i in range(HEADS + 2):
                if i < HEADS:
                    dve.wait_ge(s_mm, i + 1)
                    if i >= 2:
                        dve.wait_ge(pt_mm, i - 1)
                    pr, st = probs[:, i % 2, :], stat[:, i % 2, :]
                    link(nc.vector.tensor_tensor(pr, bank[i % 2][:, 0:QW], mask[:, :], ALU.add))
                    link(nc.vector.reduce_max(st[:, 0:1], pr[:, 0:P], AX.X))
                    link(nc.vector.reduce_max(st[:, 1:2], pr[:, P:QW], AX.X))
                    nc.vector.tensor_scalar(st[:, 2:4], st[:, 0:2], -SCALE, None, ALU.mult).then_inc(max_ready, 1)
                    dve.wait_ge(exp_ready, i + 1)
                    link(nc.vector.reciprocal(st[:, 6:8], st[:, 4:6]))
                    nc.vector.tensor_scalar(pr[:, 0:P], pr[:, 0:P], st[:, 6:7], None, ALU.mult)
                    nc.vector.tensor_scalar(pr[:, P:QW], pr[:, P:QW], st[:, 7:8], None, ALU.mult).then_inc(probs_ready, 1)
                h = i - 2
                if h >= 0:
                    dve.wait_ge(o_hi, h + 1)
                    nc.vector.tensor_tensor(attnT[:, h, SEQ:], bank[4 + h % 2][:, 0:SEQ], attnT[:, h, 0:SEQ].bitcast(F32),
                                            ALU.subtract).then_inc(attn_ready, 1)
            for o in range(PT):
                dve.wait_ge(mix_hi, o + 1)
                nc.vector.scalar_tensor_tensor(out=poolT[:, o, SEQ:], in0=bank[6 + o % 2][:, 0:SEQ],
                                               scalar=par[:, PC_PSCALE + o:PC_PSCALE + o + 1],
                                               in1=poolT[:, o, 0:SEQ].bitcast(F32), op0=ALU.mult,
                                               op1=ALU.subtract).then_inc(pool_ready, 1)
            with dve.Fori(0, 4) as it:
                step.enter(it, 12)
                for g in range(2):
                    rest(PH_GATE, it, g)
                    head(PH_GATE, it + g, 1 - g, (it + (PH_GATE.ada0 + 1), it + ADA_SH2, 4) if g == 0 else None)
                    sums(PH_GATE, it, g, lambda ft: gates[:, bass.ds(it * GT + (g * DT + ft), 1), :].rearrange("p a n -> p (a n)"), half_a)
                step.leave(4)
            dve.wait_ge(gate_ready, 2 * DT)
            with dve.Fori(0, 4) as it:
                step.enter(it, 2 * GT)
                for g in range(2):
                    head(PH_BR, it + g, 1 - g)
                    y = y_attn if g == 0 else y_sum

                    def gated(ft):
                        gate = gates[:, bass.ds(it * GT + (g * DT + ft), 1), :].rearrange("p a n -> p (a n)")
                        link(nc.vector.tensor_tensor(y[:, ft, :], y[:, ft, :], gate, ALU.mult))
                        if g == 1:
                            nc.vector.tensor_tensor(y[:, ft, :], y[:, ft, :], y_attn[:, ft, :], ALU.add).then_inc(merge_sum, 1)

                    sums(PH_BR, it, g, lambda ft: y[:, ft, :], half_a, gated)
                for ft in range(GT):
                    dve.wait_ge(merge_hi, it * GT + (ft + 1))
                    t = bass.ds(it * GT + ft, 1)
                    nc.vector.tensor_tensor(hT[:, t, SEQ:], y_sum[:, ft:ft + 1, :], hT[:, t, 0:SEQ].bitcast(F32),
                                            ALU.subtract).then_inc(merged_ready, 1)
                dve.wait_ge(merged_ready, it * GT + GT)
                step.leave(4)
            link(nc.vector.memset(ss_x[:, :], 0.0))
            with dve.Fori(0, 2) as it:
                step.enter(it, 2 * 12)
                for g in range(2):
                    rest(PH_WO, it, g)
                    head(PH_WO, it + g, 1 - g,
                         (it * 2 + (PH_WO.ada0 + g + 1), it * 2 + (ADA_G1 + g), 4 * (1 - g)))

                    def residual(ft):
                        t = bass.ds(it * (2 * GT) + (g * GT + ft), 1)
                        if ft == 0:
                            dve.wait_ge(mod_ready, it * 2 + (PH_WO.ada0 + g + 1))
                        nc.vector.scalar_tensor_tensor(
                            out=xT[:, t, :], in0=y_sum[:, ft:ft + 1, :],
                            scalar=mod[:, bass.ds(it * (2 * GT) + (ADA_G1 * GT + g * GT + ft), 1)],
                            in1=xT[:, t, :], op0=ALU.mult, op1=ALU.add).then_inc(x1_ready, 1)

                    sums(PH_WO, it, g, lambda ft: y_sum[:, ft, :], half_a, residual)
                    for ft in range(GT):
                        dve.wait_ge(sq1_ready, it * (2 * GT) + (g * GT + ft + 1))
                        nc.vector.tensor_tensor(ss_x[:, :], ss_x[:, :], sq_x1[:, ft, :], ALU.add).then_inc(ss_ready, 1)
                        dve.wait_ge(ss_ready, it * (2 * GT) + (g * GT + ft + 1))
                step.leave(2)
            dve.wait_ge(mod_ready, ADA_G2)
            norm(DT, PC_GFFN, ADA_SC2 * GT, t_x1)

            dve.wait_ge(spilled, 16)
            link(nc.vector.memset(up_pad[:, :, 0:2], 0.0))

            def taps(it, g):
                dst = conv_a if g == 0 else conv_b_

                def tap(ft, j):
                    w = par[:, bass.ds(it * GT + (PC_CONV[j] + g * FT + ft), 1)]
                    return nc.vector.scalar_tensor_tensor(out=dst[:, ft, :], in0=up_pad[:, ft, j:j + SEQ], scalar=w,
                                                          in1=dst[:, ft, :], op0=ALU.mult, op1=ALU.add)

                for ft in range(GT):
                    dve.wait_ge(tap2_ready, it * (2 * GT) + (g * GT + ft + 1))
                    step.inc(tap(ft, 1))
                for ft in range(GT):
                    dve.wait_ge(dve_step, step.value() - (GT - 1 - ft))
                    tap(ft, 0).then_inc(taps_ready, 1)
                dve.wait_ge(taps_ready, it * (2 * GT) + (g + 1) * GT)

            with dve.Fori(0, 11) as it:
                step.enter(it, 2 * GT)
                for g in range(2):
                    rest(PH_UP, it, g)
                    head(PH_UP, it + g, 1 - g)
                    sums(PH_UP, it, g, lambda ft: up_pad[:, ft, 2:], half_b)
                    taps(it, g)
                for ft in range(GT):
                    dve.wait_ge(silu_a, it * GT + (ft + 1))
                    nc.vector.tensor_tensor(conv_b_[:, ft, :], conv_b_[:, ft, :], conv_a[:, ft, :],
                                            ALU.mult).then_inc(glu_ready, 1)
                for ft in range(GT):
                    dve.wait_ge(act_hi, it * GT + (ft + 1))
                    t = bass.ds(it * GT + ft, 1)
                    nc.vector.tensor_tensor(actT[:, t, SEQ:], conv_b_[:, ft:ft + 1, :], actT[:, t, 0:SEQ].bitcast(F32),
                                            ALU.subtract).then_inc(act_ready, 1)
                dve.wait_ge(act_ready, it * GT + GT)
                step.leave(11)

            for it in range(2):
                for g in range(2):
                    G = 2 * it + g
                    rest(PH_DOWN, it, g)
                    store = (PH_DOWN.ada0 + G + 1, ADA_G2 + G, 4 * (1 - g))
                    if G < 3:
                        head(PH_DOWN, it + g, 1 - g, store)
                    else:
                        mod_store(*store)

                    def residual2(ft):
                        t = G * GT + ft
                        if t == 0:
                            dve.wait_ge(x1_back, 16)
                        if ft == 0:
                            dve.wait_ge(mod_ready, PH_DOWN.ada0 + G + 1)
                        nc.vector.scalar_tensor_tensor(
                            out=x2T[:, t, :], in0=conv_a[:, ft, :], scalar=mod[:, ADA_G2 * GT + t:ADA_G2 * GT + t + 1],
                            in1=x2T[:, t, :], op0=ALU.mult, op1=ALU.add).then_inc(x2_ready, 1)

                    if G:
                        dve.wait_ge(x2_ready, G * GT)
                    sums(PH_DOWN, it, g, lambda ft: conv_a[:, ft, :], half_b, residual2)
            for G in range(4):
                dve.wait_ge(out_mm, G + 1)
                nc.vector.tensor_copy(out_tok[:, G, 1, :], bank[2 * G + 1][:, :]).then_inc(out_copied, 1)

        @block.tensor
        def _(pe):
            def main_chunk(ph, it, g, c, x, value=False):
                n_chunks, sc = ph.body_chunks // 2, ph.chunk_slot(g, c)
                pos = ph.pos(g, "main", c * CHUNK_T // LOAD_T)
                pe.wait_ge(half_used, ph.used(it, pos, c % 2 + 1))
                for t in range(CHUNK_T):
                    k = c * CHUNK_T + t
                    first, final = k == 0, k == n_chunks * CHUNK_T - 1
                    if value:
                        for tok in range(2):
                            b = bank[4 * g + tok]
                            hi, lo = (x[:, k, o + tok * P:o + (tok + 1) * P] for o in (0, SEQ))
                            nc.tensor.matmul(b[:, :], hi, w_hi[:, sc, t, :], start=first, stop=False)
                            nc.tensor.matmul(b[:, :], hi, w_lo[:, sc, t, :], start=False, stop=False)
                            last = nc.tensor.matmul(b[:, :], lo, w_hi[:, sc, t, :], start=False, stop=final)
                        continue
                    for ft in range(GT):
                        b = bank[4 * g + ft]
                        hi, lo = (w[:, sc, t, ft * P:(ft + 1) * P] for w in (w_hi, w_lo))
                        if t == 0:
                            nc.tensor.matmul(b[:, :], hi, x[:, k, :], start=first, stop=False)
                            last = nc.tensor.matmul(b[:, 0:SEQ], lo, x[:, k, 0:SEQ], start=False, stop=False)
                        else:
                            nc.tensor.matmul(b[:, 0:SEQ], lo, x[:, k, 0:SEQ], start=False, stop=False)
                            last = nc.tensor.matmul(b[:, :], hi, x[:, k, :], start=False, stop=final)
                last.then_inc(chunk_used, 1)

            def ada_reduce(b):
                for ft in range(GT):
                    last = nc.tensor.matmul(bank[b][:, ft:ft + 1], ada_acc[:, ft * P:(ft + 1) * P], ones[:, 0:1],
                                            start=True, stop=True)
                last.then_inc(ada_sum, 1)

            def group(ph, it, g, x, value=False, ready=None):
                if ph is not PH_U:
                    pe.wait_ge(sum_ready, it * (2 * GT) + (ph.group0 + g - 1) * GT)
                pe.wait_ge(mod_ready, it * sum(ph.ada) + (ph.ada0 + sum(ph.ada[:g])))
                n_chunks = ph.body_chunks // 2
                for c in range(n_chunks):
                    if ready:
                        ready(c)
                    if c == n_chunks - 1 and ph.ada[g]:
                        pe.wait_ge(half_used, ph.used(it, ph.pos(g, "ada", 3), 2))
                        if ph is not PH_U:
                            pe.wait_ge(sum_ready, it * (2 * GT) + (ph.group0 + g) * GT)
                        ada_reduce(4 * (1 - g))
                    main_chunk(ph, it, g, c, x, value)

            pe.wait_ge(square_in, 16)
            pe.wait_ge(par_in, 12 * 16)
            nc.tensor.transpose(bank[7][:, 0:P], par_rows[:, 0, :], ident).then_inc(par_mm, 1)
            pe.wait_ge(x_in, 16)
            for b in range(8):
                if b == 7:
                    pe.wait_ge(par_ready, 1)
                for n in range(4):
                    t, tok = 2 * b + n // 2, n % 2
                    last = nc.tensor.transpose(bank[b][:, n * P:(n + 1) * P], x_tok[:, tok, t * P:(t + 1) * P], ident)
                last.then_inc(xt_mm, 1)
            pe.wait_ge(xt_ready, 8)
            for n in range(1, 6):
                r = PBLOCK_ROWS[n]
                b, o = (bank[5], (n - 1) * P) if n < 5 else (bank[6], 0)
                last = nc.tensor.transpose(b[:, o:o + r], par_rows[0:r, n, :], ident[0:r, 0:r])
            last.then_inc(par_mm, 1)
            pe.wait_ge(sqx_used, 8)
            nc.tensor.matmul(bank[4][:, 0:SEQ], ones, ss_x[:, :], start=True, stop=True).then_inc(ss_mm, 1)
            for it in range(8):
                pe.wait_ge(half_used, it * 8 + 8)
                if it:
                    pe.wait_ge(mod_ready, it)
                ada_reduce(0)

            group(PH_U, 0, 0, hT, ready=lambda c: pe.wait_ge(h_ready, (c + 1) * CHUNK_T))
            group(PH_U, 0, 1, hT)
            with pe.Fori(0, 2) as it:
                for g in range(2):
                    group(PH_QK, it, g, hT)
            for g in range(2):
                group(PH_V, 0, g, hT, value=True)

            pe.wait_ge(const_in, 48)
            pe.wait_ge(sum_ready, PH_V.group_end * GT)
            for i in range(2 * HEADS):
                pe.wait_ge(rope_in, 2 * i + 2)
                if i >= 8:
                    pe.wait_ge(rope_out, i - 7)
                nc.tensor.matmul(bank[i % 8][:, 0:SEQ], rope_c[:, 2 * SEQ:], tg[:, i % 4, :], start=True, stop=True)
                nc.tensor.matmul(bank[i % 8][:, SEQ:], ones, sq[:, i % 4, :], start=True, stop=True).then_inc(rope_mm, 1)
            pe.wait_ge(rope_out, 2 * HEADS)
            for i in range(HEADS + 2):
                if i < HEADS:
                    b = bank[i % 2]
                    if i >= 2:
                        pe.wait_ge(max_ready, i - 1)
                    nc.tensor.matmul(b[:, 0:P], qk[:, i, 0:P], qk[:, HEADS + i, 0:P], start=True, stop=True)
                    nc.tensor.matmul(b[:, P:QW], qk[:, i, P:SEQ], qk[:, HEADS + i, :], start=True, stop=True).then_inc(s_mm, 1)
                h = i - 1
                if 0 <= h < HEADS:
                    pe.wait_ge(probs_ready, h + 1)
                    if h >= 2:
                        pe.wait_ge(pt_ready, h - 1)
                    for n in range(3):
                        last = nc.tensor.transpose(bank[2 + h % 2][:, n * P:(n + 1) * P],
                                                   probs[:, h % 2, n * P:(n + 1) * P], ident)
                    last.then_inc(pt_mm, 1)
                h = i - 2
                if h >= 0:
                    b = bank[4 + h % 2]
                    pe.wait_ge(pt_ready, h + 1)
                    if h >= 2:
                        pe.wait_ge(attn_ready, h - 1)
                    nc.tensor.matmul(b[:, 0:SEQ], v_tok[:, 0, h * HD:(h + 1) * HD], probsT[:, h % 2, 0:SEQ],
                                     start=True, stop=False)
                    nc.tensor.matmul(b[:, P:SEQ], v_tok[:, 1, h * HD:(h + 1) * HD], probsT[:, h % 2, SEQ:QW],
                                     start=False, stop=True).then_inc(o_mm, 1)
            pe.wait_ge(wp_in, 16)
            pe.wait_ge(d_ready, 1)
            for o in range(PT):
                if o >= 2:
                    pe.wait_ge(pool_ready, o - 1)
                for t in range(2):
                    last = nc.tensor.matmul(bank[6 + o % 2][:, 0:SEQ], w_pool[:, o // 2, t, (o % 2) * P:(o % 2 + 1) * P],
                                            u_pad[:, o // 2 * 2 + t, PAD:], start=t == 0, stop=t == 1)
                last.then_inc(mix_mm, 1)

            pe.wait_ge(attn_ready, HEADS)
            pe.wait_ge(pool_ready, PT)
            with pe.Fori(0, 4) as it:
                for g in range(2):
                    group(PH_GATE, it, g, hT)
            with pe.Fori(0, 4) as it:
                group(PH_BR, it, 0, attnT)
                group(PH_BR, it, 1, poolT)
            with pe.Fori(0, 2) as it:
                group(PH_WO, it, 0, hT, ready=lambda c: pe.wait_ge(merged_ready, DT - GT if c < 6 else DT) if c in (0, 6) else None)
                group(PH_WO, it, 1, hT)
            pe.wait_ge(ss_ready, DT)
            nc.tensor.matmul(bank[0][:, 0:SEQ], ones, ss_x[:, :], start=True, stop=True).then_inc(ss_mm, 1)
            with pe.Fori(0, 11) as it:
                group(PH_UP, it, 0, hT, ready=lambda c: pe.wait_ge(h_ready, DT + (c + 1) * CHUNK_T))
                group(PH_UP, it, 1, hT)
            with pe.Fori(0, 2) as it:
                group(PH_DOWN, it, 0, actT, ready=lambda c: pe.wait_ge(act_ready, FT - GT if c < 20 else FT) if c in (0, 20) else None)
                group(PH_DOWN, it, 1, actT)
            pe.wait_ge(sum_ready, PH_DOWN.group_end * GT)
            for G in range(4):
                pe.wait_ge(x2_ready, (G + 1) * GT)
                for tok in range(2):
                    for ft in range(GT):
                        last = nc.tensor.transpose(bank[2 * G + tok][:, ft * P:(ft + 1) * P],
                                                   x2T[:, G * GT + ft, tok * P:(tok + 1) * P], ident)
                last.then_inc(out_mm, 1)


_INS = ["x", "c", "w_ada", "b_ada", "norm_mix_g", "w_in", "q_norm_g", "k_norm_g", "w_pool_grp", "pool_scale",
        "w_attn_br", "w_pool_br", "w_gate", "b_gate", "w_o", "norm_ffn_g", "w_up", "conv_w", "conv_b", "w_down"]


def shape_constants():
    square = np.stack([np.eye(P, dtype=np.float32), np.ones((P, P), np.float32)], 1)
    half = HD // 2
    inv = np.float32(10000.0) ** (-np.arange(half, dtype=np.float32) / np.float32(half))
    ang = (np.arange(SEQ, dtype=np.float32)[None, :] * inv.astype(np.float32)[:, None]).astype(np.float32)
    turn = np.zeros((P, P), np.float32)
    turn[np.arange(half) + half, np.arange(half)] = -1.0
    turn[np.arange(half), np.arange(half) + half] = 1.0
    rope = np.concatenate([np.tile(np.cos(ang), (2, 1)), np.tile(np.sin(ang), (2, 1)), turn], 1).astype(np.float32)
    later = np.where(np.arange(P)[None, :] > np.arange(P)[:, None], np.float32(NEG), np.float32(0))
    mask = np.concatenate([later, np.zeros((P, P), np.float32), later], 1).astype(np.float32)
    counts = np.stack([np.minimum(np.arange(SEQ) + 1, w) for w in POOL_WINDOWS])
    invcnt = np.broadcast_to((1.0 / counts).astype(np.float32), (P, 4, SEQ)).copy()
    return {"k_square": square, "k_rope": rope, "k_mask": mask, "k_invcnt": invcnt}


def kernel(**inputs):
    import concourse.bacc as _bacc
    from concourse.bass_utils import run_bass_kernel_spmd as _run

    nc = _bacc.Bacc("TRN2", target_bir_lowering=False, num_devices=1)
    arrays, args = {}, []
    given = {name: np.ascontiguousarray(inputs[name]) for name in _INS}
    given.update(shape_constants())
    for name, a in given.items():
        arrays[f"in_{name}"] = a
        args.append(nc.dram_tensor(f"in_{name}", a.shape, mybir.dt.from_np(a.dtype), kind="ExternalInput").ap())
    args.append(nc.dram_tensor("out", (1, SEQ, D), F32, kind="ExternalOutput").ap())
    args.append(nc.dram_tensor("x1_spill", (P, DT * SEQ), F32, kind="Internal").ap())
    build_block(nc, *args)
    r = _run(nc, [arrays], core_ids=[0])
    return r.results[0]["out"]
```

```python
from contextlib import ExitStack

import concourse.bass as bass
import numpy as np
from concourse import mybir

F32 = mybir.dt.float32
F32R = mybir.dt.float32r
ALU = mybir.AluOpType
ACT = mybir.ActivationFunctionType
AX = mybir.AxisListType

P = 128
SEQ = 256
D = 2048
DT = D // P
HEADS = 8
HD = 128
POOL_WINDOWS = (2, 4, 8, 16)
PT = 1024 // P
FF = 5632
FT = FF // P
EPS = 1e-6
NEG = -1e30
SCALE = float(HD) ** -0.5
COLS = 512
GT = COLS // P
LOAD_T = 4
CHUNK_T = 2
RAW_SLOTS = 4
CHUNK_SLOTS = 4
PAD = max(POOL_WINDOWS)
QW = P + SEQ

FF2T = 2 * FT
PBLOCK_ROWS = [128, 58, FF2T, FF2T, FF2T, FF2T]
PBLOCK_COL = [sum(PBLOCK_ROWS[:n]) for n in range(7)]
PC_C, PC_GMIX, PC_BADA = 0, 16, 32
PC_GFFN, PC_PSCALE, PC_BGATE, PC_QG, PC_KG = 128, 144, 152, 184, 185
PC_CONV = PBLOCK_COL[2:6]

ADA_SH1, ADA_SC1, ADA_G1, ADA_SH2, ADA_SC2, ADA_G2 = 0, 4, 8, 12, 16, 20


class Phase:

    def __init__(self, before, bodies, loads, ada, lead=2, groups=2):
        self.loads, self.ada, self.lead, self.groups = loads, ada, lead, groups
        self.chunks = loads * LOAD_T // CHUNK_T
        self.body_loads = groups * loads + LOAD_T * ada
        self.body_chunks = groups * self.chunks
        self.load0 = before.load_end if before else 8 * 4
        self.chunk0 = before.chunk_end if before else 0
        self.group0 = before.group_end if before else 0
        self.ada0 = before.ada_end if before else 8
        self.load_end = self.load0 + bodies * self.body_loads
        self.chunk_end = self.chunk0 + bodies * self.body_chunks
        self.group_end = self.group0 + bodies * groups
        self.ada_end = self.ada0 + bodies * ada

    def group(self, it, g):
        return it * self.groups + (self.group0 + g)

    def chunk(self, it, g, c):
        return it * self.body_chunks + (self.chunk0 + g * self.chunks + c)

    def chunk_slot(self, g, c):
        return (g * self.chunks + c) % CHUNK_SLOTS

    def order(self, g):
        seq = [("main", m) for m in range(self.loads)]
        n = self.lead
        if self.ada == 1 and self.groups == 4:
            seq = seq[:2] + [("ada", g)] + seq[2:]
        elif self.ada == 1:
            seq = seq[:n] + [("ada", 2 * g)] + seq[n:n + 1] + [("ada", 2 * g + 1)] + seq[n + 1:]
        if self.ada == 2:
            seq = seq[:n] + [("ada", 0), ("ada", 1)] + seq[n:n + 1] + [("ada", 2), ("ada", 3)] + seq[n + 1:]
        return seq

    def pos(self, g, kind, n):
        return self.body_loads // self.groups * g + self.order(g).index((kind, n))

    def ada_before(self, it, g):
        return it * self.ada + (self.ada0 + (g if self.ada == 2 else 0))

    def reduces(self, g):
        return self.ada == 2 or (self.ada == 1 and g == self.groups - 1)

    def load(self, it, pos):
        return it * self.body_loads + (self.load0 + pos)

    def slot(self, it, pos):
        if isinstance(it, int):
            return self.load(it, pos) % RAW_SLOTS
        assert self.load0 % RAW_SLOTS == 0 and self.body_loads % RAW_SLOTS == 0
        return pos % RAW_SLOTS

    def landed(self, it, pos):
        if isinstance(it, int):
            return 16 * (self.load(it, pos) // RAW_SLOTS + 1)
        return it * (16 * self.body_loads // RAW_SLOTS) + 16 * ((self.load0 + pos) // RAW_SLOTS + 1)

    def used(self, it, pos, half):
        return it * (2 * self.body_loads) + (2 * (self.load0 + pos) + half)


PH_U = Phase(None, 1, 4, 1)
PH_QK = Phase(PH_U, 2, 4, 1)
PH_V = Phase(PH_QK, 1, 4, 1)
PH_GATE = Phase(PH_V, 4, 4, 1)
PH_BR = Phase(PH_GATE, 2, 2, 1, groups=4)
PH_WO = Phase(PH_BR, 2, 4, 1, lead=3)
PH_UP = Phase(PH_WO, 11, 4, 0)
PH_DOWN = Phase(PH_UP, 2, 11, 2, lead=3)


class Tally:

    def __init__(self, sem):
        self.sem, self.n, self.extra = sem, 0, None

    def inc(self, instruction):
        instruction.then_inc(self.sem, 1)
        self.n += 1

    def value(self):
        return self.n if self.extra is None else self.extra + self.n

    def enter(self, it, per, first=0):
        self.start, self.per = self.n, per
        self.extra = it * per + (-first * per)

    def leave(self, count):
        assert self.n - self.start == self.per, (self.n - self.start, self.per)
        self.n = self.start + count * self.per
        self.extra = None


def build_block(nc, x, c, w_ada, b_ada, norm_mix_g, w_in, q_norm_g, k_norm_g, w_pool_grp,
                pool_scale, w_attn_br, w_pool_br, w_gate, b_gate, w_o, norm_ffn_g, w_up,
                conv_w, conv_b, w_down, k_square, k_rope, k_mask, k_invcnt, out, x1_spill):
    ctx = ExitStack()
    with ctx:
        cursor = [nc.sbuf_base + (-nc.sbuf_base) % 64]

        def at(name, shape, dt, offset):
            return nc.alloc_sbuf_tensor_at(name, shape, dt, offset=offset)

        def keep(name, shape, dt=F32):
            t = at(name, shape, dt, cursor[0])
            cursor[0] += int(np.prod(shape[1:])) * 4
            cursor[0] += (-cursor[0]) % 32
            return t

        def sem(name):
            return ctx.enter_context(nc.semaphore(name))

        raw = keep("raw", [P, RAW_SLOTS, LOAD_T, COLS])
        w_hi = keep("w_hi", [P, CHUNK_SLOTS, CHUNK_T, COLS], F32R)
        w_lo = keep("w_lo", [P, CHUNK_SLOTS, CHUNK_T, COLS], F32R)
        square = keep("square", [P, 2, P])
        par = keep("par", [P, PBLOCK_COL[6]])
        mod = keep("mod", [P, 6 * DT])
        silu_c = keep("silu_c", [P, DT])
        scale_a = keep("scale_a", [P, DT])
        eps = keep("eps", [P, 1])
        ada_acc = keep("ada_acc", [P, 2, COLS])
        rsq = keep("rsq", [P, 2 * HEADS])
        h0 = cursor[0]
        hT = keep("hT", [P, DT, 2 * SEQ], F32R)
        x0 = cursor[0]
        xT = keep("xT", [P, DT, SEQ])
        cursor[0] += 64
        big = cursor[0]
        actT = keep("actT", [P, FT, 2 * SEQ], F32R)
        ident, ones = square[:, 0, :], square[:, 1, :]

        def early(name, shape, offset, dt=F32):
            assert offset + int(np.prod(shape[1:])) * 4 <= FT * 2 * SEQ * 4
            return at(name, shape, dt, big + offset)

        attnT = early("attnT", [P, HEADS, 2 * SEQ], 0, F32R)
        poolT = early("poolT", [P, PT, 2 * SEQ], 16384, F32R)
        gates = early("gates", [P, 2 * DT, SEQ], 32768)
        qk = early("qk", [P, HEADS, 2, SEQ], 49152)
        v_tok = early("v_tok", [P, 2, HEADS * HD], 65536)
        u_pad = early("u_pad", [P, PT, PAD + SEQ], 73728)
        half_a = early("half_a", [P, GT, SEQ], 82432)
        rs_x = early("rs_x", [P, 1, SEQ], 87552)
        mask = early("mask", [P, QW], 88576)
        x_tok = early("x_tok", [P, 2, D], 0)
        par_rows = early("par_rows", [P, 6, P], 16384)
        sq_x = early("sq_x", [P, 2, 2 * SEQ], 20480)
        t_x = early("t_x", [P, 2, SEQ], 26624)
        acc_shift = early("acc_shift", [P, 2, COLS], 49152)
        pool_s = [early(f"pool_s{n}", [P, PT, PAD + SEQ], n * 8704) for n in range(2)]
        tg = early("tg", [P, GT, SEQ], 17408)
        sq = early("sq", [P, GT, SEQ], 21504)
        rb = early("rb", [P, GT, SEQ], 25600)
        diag = early("diag", [P, 2 * GT, P], 29696)
        root = early("root", [P, 2 * GT], 33792)
        rsk = early("rsk", [P, 2 * GT], 33824)
        rope_c = early("rope_c", [P, 2 * SEQ + P], 36864)
        invcnt = early("invcnt", [P, 4, SEQ], 40960)
        probs = at("probs", [P, 2, QW], F32, x0)
        probsT = at("probsT", [P, 2, QW], F32, x0 + 3072)
        q_st = at("q_st", [P, 2, SEQ], F32, x0 + 6144)
        v_st = at("v_st", [P, 2, 2, HD], F32, x0 + 8192)
        wp_st = at("wp_st", [P, 2, 2, P], F32, x0 + 10240)
        stat = at("stat", [P, 2, 8], F32, x0 + 12288)
        y_attn = early("y_attn", [P, GT, SEQ], 65536)
        y_sum = early("y_sum", [P, GT, SEQ], 69632)
        sq_x1 = early("sq_x1", [P, GT, SEQ], 0)
        ss_x1 = early("ss_x1", [P, GT, SEQ], 4096)
        t_x1 = early("t_x1", [P, 2, SEQ], 8192)
        half_b = at("half_b", [P, GT, SEQ], F32, x0)
        up_pad = at("up_pad", [P, GT, 2 + SEQ], F32, x0 + 4096)
        conv_a = at("conv_a", [P, GT, SEQ], F32, x0 + 4096 + 4128)
        conv_b_ = at("conv_bb", [P, GT, SEQ], F32, x0 + 8192 + 4128)
        x2T = at("x2T", [P, DT, SEQ], F32, h0)
        x2_even = conv_b_
        out_tok = at("out_tok", [P, 4, 2, COLS], F32, h0 + 16384)

        psum = ctx.enter_context(nc.psum_tensor("psum", [P, 8, 512], F32))
        bank = [psum[:, n, :] for n in range(8)]

        x_in, par_in, square_in, const_in = sem("x_in"), sem("par_in"), sem("square_in"), sem("const_in")
        par_in2 = sem("par_in2")
        raw_full = [sem(f"raw_full{n}") for n in range(RAW_SLOTS)]
        half_used = sem("half_used")
        hi_ready = sem("hi_ready")
        chunk_used = sem("chunk_used")
        half_ready = sem("half_ready")
        sum_ready = sem("sum_ready")
        ada_sum = sem("ada_sum")
        mod_ready = sem("mod_ready")
        dve_step = sem("dve_step")
        act_step = sem("act_step")
        pool_step = sem("pool_step")
        xt_mm, xt_ready = sem("xt_mm"), sem("xt_ready")
        par_mm, par_ready = sem("par_mm"), sem("par_ready")
        silu_ready = sem("silu_ready")
        eps_ready = sem("eps_ready")
        sqx_ready, sqx_used = sem("sqx_ready"), sem("sqx_used")
        ss_ready, ss_mm, rt_ready, rs_ready = sem("ss_ready"), sem("ss_mm"), sem("rt_ready"), sem("rs_ready")
        t_ready, h_hi, h_ready = sem("t_ready"), sem("h_hi"), sem("h_ready")
        d_ready = sem("d_ready")
        rope_in = sem("rope_in")
        rope_mm = sem("rope_mm")
        rope_root = sem("rope_root")
        rope_sin = sem("rope_sin")
        rope_out = sem("rope_out")
        k_mm, k_ready = sem("k_mm"), sem("k_ready")
        stage_ready = sem("stage_ready")
        wp_in = [sem(f"wp_in{n}") for n in range(2)]
        s_mm, max_ready, exp_ready, probs_ready = sem("s_mm"), sem("max_ready"), sem("exp_ready"), sem("probs_ready")
        pt_mm, pt_ready, o_mm, o_hi, attn_ready = sem("pt_mm"), sem("pt_ready"), sem("o_mm"), sem("o_hi"), sem("attn_ready")
        mix_mm, mix_hi, pool_ready = sem("mix_mm"), sem("mix_hi"), sem("pool_ready")
        gate_ready = sem("gate_ready")
        merge_sum, merge_hi, merged_ready = sem("merge_sum"), sem("merge_hi"), sem("merged_ready")
        x1_ready, sq1_ready = sem("x1_ready"), sem("sq1_ready")
        tap2_ready, taps_ready, silu_a = sem("tap2_ready"), sem("taps_ready"), sem("silu_a")
        glu_ready, act_hi, act_ready = sem("glu_ready"), sem("act_hi"), sem("act_ready")
        x_spilled, x_back, spilled, x1_back = sem("x_spilled"), sem("x_back"), sem("spilled"), sem("x1_back")
        x2_ready, out_mm, stored = sem("x2_ready"), sem("out_mm"), sem("stored")
        out_copied = [sem(f"out_copied{n}") for n in range(2)]

        def tiles(w):
            return w.rearrange("(t p) n -> p t n", p=P)

        def rows(w, t0, col):
            return tiles(w)[:, t0:t0 + LOAD_T, bass.ds(col, COLS)]

        def flat(w):
            return w.rearrange("(t p) -> t p", p=P)

        block = ctx.enter_context(nc.Block())

        @block.sync
        def _(sp):
            def load(src, it, ph, pos):
                slot = ph.slot(it, pos)
                sp.wait_ge(half_used, ph.used(it, pos - RAW_SLOTS, 2))
                sp.dma_start(raw[:, slot, :, :], src).then_inc(raw_full[slot], 16)

            def body(ph, it, mains, adas):
                pos = 0
                for g in range(ph.groups):
                    for kind, n in ph.order(g):
                        w, col = mains[g] if kind == "main" else (w_ada[0], adas[g % len(adas)] * COLS)
                        load(rows(w, n * LOAD_T, col), it, ph, pos)
                        pos += 1

            sp.dma_start(square[:, :, :], k_square).then_inc(square_in, 16)
            for r0, blk, src in ((0, 0, flat(c[0])), (16, 0, flat(norm_mix_g[0])), (32, 0, flat(b_ada[0]))):
                sp.dma_start(par_rows[r0:r0 + src.shape[0], blk, :], src).then_inc(par_in, 16)
            for G, w in enumerate(w for it in range(GT) for w in (ADA_SC1 + it, ADA_SH1 + it)):
                for q in range(RAW_SLOTS):
                    if G > 0:
                        sp.wait_ge(half_used, 2 * ((G - 1) * RAW_SLOTS + q + 1))
                    sp.dma_start(raw[:, q, :, :], rows(w_ada[0], q * LOAD_T, w * COLS)).then_inc(raw_full[q], 16)
            sp.dma_start(rope_c[:, :], k_rope).then_inc(const_in, 16)
            sp.dma_start(mask[:, :], k_mask).then_inc(const_in, 16)
            sp.dma_start(invcnt[:, :, :], k_invcnt).then_inc(const_in, 16)
            body(PH_U, 0, [(w_in[0], 3072), (w_in[0], 3584)], [ADA_SC2])
            with sp.Fori(0, 2) as it:
                body(PH_QK, it, [(w_in[0], it * COLS), (w_in[0], it * COLS + 1024)], [it + (ADA_SC2 + 1)])
            body(PH_V, 0, [(w_in[0], 2048), (w_in[0], 2560)], [ADA_SC2 + 3])
            with sp.Fori(0, 4) as it:
                body(PH_GATE, it, [(w_gate[0], it * COLS), (w_gate[0], it * COLS + D)], [it + ADA_SH2])
            with sp.Fori(0, 2) as it:
                body(PH_BR, it, [(w, it * (2 * COLS) + n * COLS) for n in range(2) for w in (w_attn_br[0], w_pool_br[0])],
                     [it + ADA_G1])
            with sp.Fori(0, 2) as it:
                body(PH_WO, it, [(w_o[0], it * (2 * COLS)), (w_o[0], it * (2 * COLS) + COLS)], [it + (ADA_G1 + 2)])
            with sp.Fori(0, 11) as it:
                body(PH_UP, it, [(w_up[0], it * COLS), (w_up[0], it * COLS + FF)], [0])
            for it in range(2):
                body(PH_DOWN, it, [(w_down[0], 2 * it * COLS), (w_down[0], (2 * it + 1) * COLS)],
                     [ADA_G2 + 2 * it, ADA_G2 + 2 * it + 1])

        @block.gpsimd
        def _(pool):
            step = Tally(pool_step)

            def link(ins):
                step.inc(ins)
                pool.wait_ge(pool_step, step.value())

            nc.gpsimd.memset(eps[:, :], EPS).then_inc(eps_ready, 1)
            pool.wait_ge(xt_mm, 8)
            pool.wait_ge(par_mm, 2)
            for t in (u_pad, pool_s[0], pool_s[1]):
                link(nc.gpsimd.memset(t[:, :, 0:PAD], 0.0))
            pool.wait_ge(sum_ready, 2)
            pool.wait_ge(const_in, 48)
            src = u_pad
            for n, w in enumerate(POOL_WINDOWS):
                dst, other, t0 = pool_s[n % 2], pool_s[(n + 1) % 2], 2 * n
                link(nc.gpsimd.tensor_tensor(dst[:, t0:, PAD:], src[:, t0:, PAD:],
                                             src[:, t0:, PAD - w // 2:PAD + SEQ - w // 2], ALU.add))
                for t in (t0, t0 + 1):
                    link(nc.gpsimd.tensor_tensor(other[:, t, PAD:], dst[:, t, PAD:], invcnt[:, n, :], ALU.mult))
                    last = nc.gpsimd.tensor_tensor(u_pad[:, t, PAD:], other[:, t, PAD:], u_pad[:, t, PAD:], ALU.subtract)
                    if n < len(POOL_WINDOWS) - 1 or t == t0:
                        link(last)
                src = dst
            last.then_inc(d_ready, 1)
            pool.wait_ge(d_ready, 1)

            def turn(r, head0, which):
                heads = [qk[:, head0 + ft, which, :] for ft in range(GT)]
                pool.wait_ge(rope_in, r + 1)
                for ft in range(GT):
                    link(nc.gpsimd.tensor_tensor(heads[ft], tg[:, ft, :], rope_c[:, 0:SEQ], ALU.mult))
                pool.wait_ge(rope_sin, r + 1)
                for ft in range(GT):
                    last = nc.gpsimd.tensor_tensor(heads[ft], heads[ft], rb[:, ft, :], ALU.add)
                last.then_inc(rope_out, 1)

            for r, (head0, which) in enumerate(((0, 0), (GT, 0), (0, 1), (GT, 1))):
                turn(r, head0, which)

            def stage(h, g):
                nc.gpsimd.tensor_copy(q_st[:, g:g + 1, :], qk[:, bass.ds(h, 1), 0, :])
                nc.gpsimd.tensor_copy(v_st[:, g, :, :], v_tok[:, :, bass.ds(h * HD, HD)]).then_inc(stage_ready, 1)

            pool.wait_ge(x_spilled, 16)
            pool.wait_ge(rope_out, 4)
            pool.wait_ge(sum_ready, PH_V.group_end)
            for g in range(2):
                stage(g, g)
            with pool.Fori(1, HEADS // 2) as it:
                for g in range(2):
                    pool.wait_ge(o_mm, it * 2 + (g - 1))
                    stage(it * 2 + g, g)

            pool.wait_ge(gate_ready, 2 * DT)
            for m in range(GT):
                for n, y in enumerate((y_attn, y_sum)):
                    pool.wait_ge(sum_ready, PH_BR.group0 + 2 * m + n + 1)
                    t = n * DT + m * GT
                    link(nc.gpsimd.tensor_tensor(y[:, :, :], y[:, :, :], gates[:, t:t + GT, :], ALU.mult))
                nc.gpsimd.tensor_tensor(y_sum[:, :, :], y_sum[:, :, :], y_attn[:, :, :], ALU.add).then_inc(merge_sum, 1)

            pool.wait_ge(chunk_used, PH_BR.chunk_end)
            nc.gpsimd.memset(ss_x1[:, :, :], 0.0).then_inc(ss_ready, 1)
            for G in range(3):
                pool.wait_ge(ss_ready, G + 1)
                pool.wait_ge(sq1_ready, G + 1)
                nc.gpsimd.tensor_tensor(ss_x1[:, :, :], ss_x1[:, :, :], sq_x1[:, :, :], ALU.add).then_inc(ss_ready, 1)

        @block.scalar
        def _(act):
            def hi_chunk(ph, it, g, c):
                pos = ph.pos(g, "main", c * CHUNK_T // LOAD_T)
                if not (ph is PH_U and g == 0 and c < CHUNK_SLOTS):
                    act.wait_ge(chunk_used, ph.chunk(it, g, c - CHUNK_SLOTS + 1))
                if c % 2 == 0:
                    act.wait_ge(raw_full[ph.slot(it, pos)], ph.landed(it, pos))
                t0 = (c % 2) * CHUNK_T
                nc.scalar.activation(w_hi[:, ph.chunk_slot(g, c), :, :], raw[:, ph.slot(it, pos), t0:t0 + CHUNK_T, :],
                                     ACT.Copy).then_inc(hi_ready, 1)

            def head(ph, it, g, after=()):
                for c in range(4):
                    hi_chunk(ph, it, g, c)
                    if c in after:
                        after[c]()

            def rest(ph, it, g, after=(), c0=4):
                for c in range(c0, ph.loads * 2):
                    hi_chunk(ph, it, g, c)
                    if c in after:
                        after[c]()

            def halves(ph, it, g, half):
                act.wait_ge(chunk_used, ph.chunk(it, g, ph.chunks))
                if not (ph is PH_U and g == 0):
                    act.wait_ge(sum_ready, ph.group(it, g))
                nc.scalar.activation(half[:, :, :], psum[:, 4 * (g % 2):4 * (g % 2) + GT, SEQ:],
                                     ACT.Copy).then_inc(half_ready, 1)

            act.dma_start(x_tok[:, :, :], x[0].rearrange("(t p) n -> p t n", p=P)).then_inc(x_in, 16)
            for r0, blk, src in ((0, 1, flat(norm_ffn_g[0])), (16, 1, flat(pool_scale[0])),
                                 (24, 1, flat(b_gate[0])), (56, 1, q_norm_g), (57, 1, k_norm_g),
                                 (0, 2, flat(conv_w[0, 0])), (0, 3, flat(conv_w[0, 1])),
                                 (0, 4, flat(conv_w[0, 2])), (0, 5, flat(conv_b[0]))):
                act.dma_start(par_rows[r0:r0 + src.shape[0], blk, :], src).then_inc(par_in2, 16)
            act.wait_ge(par_mm, 1)
            nc.scalar.activation(par[:, 0:P], bank[7][:, 0:P], ACT.Copy).then_inc(par_ready, 1)
            act.wait_ge(par_ready, 1)
            nc.scalar.activation(silu_c[:, :], par[:, PC_C:PC_C + DT], ACT.Silu).then_inc(silu_ready, 1)
            for b in range(8):
                act.wait_ge(xt_mm, b + 1)
                two = xT[:, 2 * b:2 * b + 2, :].rearrange("p t n -> p (t n)")
                nc.scalar.activation(two, bank[b][:, :], ACT.Copy).then_inc(xt_ready, 1)
                act.wait_ge(xt_ready, b + 1)
                if b >= 2:
                    act.wait_ge(sqx_used, b - 1)
                nc.scalar.activation(sq_x[:, b % 2, :], two, ACT.Square).then_inc(sqx_ready, 1)
            act.wait_ge(sqx_used, 8)
            act.wait_ge(eps_ready, 1)
            nc.scalar.activation(rs_x[:, 0, :], bank[0][:, 0:SEQ], ACT.Sqrt, bias=eps[:, 0:1], scale=1.0 / D).then_inc(rt_ready, 1)
            act.wait_ge(par_mm, 2)
            for n in range(1, 6):
                r = PBLOCK_ROWS[n]
                b, o = (bank[1], (n - 1) * P) if n < 5 else (bank[2], 0)
                last = nc.scalar.activation(par[:, PBLOCK_COL[n]:PBLOCK_COL[n] + r], b[:, o:o + r], ACT.Copy)
            last.then_inc(par_ready, 1)

            def norm_hi(first, t0, n, shift, buf):
                for i in range(n):
                    act.wait_ge(t_ready, t0 + (first + i + 1))
                    nc.scalar.activation(hT[:, bass.ds(t0 + i, 1), 0:SEQ], buf[:, i % 2:i % 2 + 1, :], ACT.Identity,
                                         bias=mod[:, bass.ds(t0 + (shift + i), 1)]).then_inc(h_hi, 1)

            with act.Fori(0, 3) as it:
                norm_hi(0, it * GT, GT, ADA_SH1 * GT, t_x)
            head(PH_U, 0, 0)
            norm_hi(0, 3 * GT, GT, ADA_SH1 * GT, t_x)
            scratch = x1_spill.rearrange("p (t n) -> p t n", n=SEQ)
            act.dma_start(scratch, xT[:, :, :]).then_inc(x_spilled, 16)

            rest(PH_U, 0, 0)
            head(PH_U, 0, 1)
            halves(PH_U, 0, 0, half_a)
            rest(PH_U, 0, 1)
            head(PH_QK, 0, 0)
            halves(PH_U, 0, 1, half_a)

            def rope_inputs(head0, which, gain):
                four = qk[:, bass.ds(head0, GT), which, :]
                act.wait_ge(d_ready, 1)
                nc.scalar.activation(tg[:, :, :], four, ACT.Copy, scale=par[:, gain:gain + 1])
                nc.scalar.activation(sq[:, :, :], four, ACT.Square).then_inc(rope_in, 1)

            def rope_rms(r, g):
                act.wait_ge(rope_mm, r + 1)
                nc.scalar.activation(root[:, :], bank[4 * (1 - g)][:, SEQ:SEQ + 2 * GT], ACT.Sqrt, bias=eps[:, 0:1],
                                     scale=1.0 / HD).then_inc(rope_root, 1)

            with act.Fori(0, 2) as it:
                rest(PH_QK, it, 0)
                head(PH_QK, it, 1)
                halves(PH_QK, it, 0, half_a)
                act.wait_ge(sum_ready, it * 2 + (PH_QK.group0 + 1))
                rope_inputs(it * GT, 0, PC_QG)
                rest(PH_QK, it, 1, after={5: lambda: rope_rms(it, 1)})
                head(PH_QK, it + 1, 0)
                halves(PH_QK, it, 1, half_a)
                act.wait_ge(rope_out, it + 1)

            def v_half(g):
                act.wait_ge(chunk_used, PH_V.chunk(0, g, PH_V.chunks))
                nc.scalar.activation(v_tok[:, 0, g * COLS:(g + 1) * COLS], bank[4 * g][:, :], ACT.Copy).then_inc(half_ready, 1)

            for g in range(2):
                if g == 0:
                    act.wait_ge(sum_ready, PH_QK.group_end)
                else:
                    act.wait_ge(rope_out, 3)
                rope_inputs(g * GT, 1, PC_KG)
                rest(PH_V, 0, g, after={4: lambda: rope_rms(2 + g, g)})
                head(PH_V if g == 0 else PH_GATE, 0, 1 - g)
                v_half(g)

            def exponentials(it, g):
                act.wait_ge(max_ready, it * 2 + (g + 1))
                nc.scalar.activation(probs[:, g, 0:P], probs[:, g, 0:P], ACT.Exp, bias=stat[:, g, 2:3],
                                     scale=SCALE, accum_out=stat[:, g, 4:5])
                nc.scalar.activation(probs[:, g, P:QW], probs[:, g, P:QW], ACT.Exp, bias=stat[:, g, 3:4],
                                     scale=SCALE, accum_out=stat[:, g, 5:6]).then_inc(exp_ready, 1)

            def pool_hi(it, g):
                act.wait_ge(mix_mm, it * 2 + (g + 1))
                o = it * 2 + g
                nc.scalar.activation(poolT[:, bass.ds(o, 1), 0:SEQ], psum[:, 4 * (1 - g) + 3:4 * (1 - g) + 4, 0:SEQ],
                                     ACT.Copy, scale=par[:, bass.ds(o + PC_PSCALE, 1)]).then_inc(mix_hi, 1)

            def probs_turned(it, g):
                act.wait_ge(pt_mm, it * 2 + (g + 1))
                nc.scalar.activation(probsT[:, g, :], bank[4 * (1 - g) + 1][:, 0:QW], ACT.Copy).then_inc(pt_ready, 1)

            def attn_hi(it, g):
                act.wait_ge(o_mm, it * 2 + (g + 1))
                nc.scalar.activation(attnT[:, bass.ds(it * 2 + g, 1), 0:SEQ],
                                     psum[:, 4 * (1 - g) + 2:4 * (1 - g) + 3, 0:SEQ], ACT.Copy).then_inc(o_hi, 1)

            def sigmoids(it, g):
                act.wait_ge(sum_ready, it * 2 + (PH_GATE.group0 + g + 1))
                for ft in range(GT):
                    t = it * GT + (g * DT + ft)
                    nc.scalar.activation(gates[:, bass.ds(t, 1), :], gates[:, bass.ds(t, 1), :], ACT.Sigmoid,
                                         bias=par[:, bass.ds(t + PC_BGATE, 1)]).then_inc(gate_ready, 1)

            with act.Fori(0, 4) as it:
                for g in range(2):
                    wp = w_pool_grp[0].rearrange("g c n -> (g c) n").rearrange("(t p) n -> p t n", p=P)
                    act.dma_start(wp_st[:, g, :, :], wp[:, bass.ds(it * 2, 2), g * P:(g + 1) * P]).then_inc(wp_in[g], 16)
                    rest(PH_GATE, it, g, after={5: lambda: exponentials(it, g), 6: lambda: pool_hi(it, g)})
                    head(PH_GATE, it + g, 1 - g, after={1: lambda: probs_turned(it, g), 2: lambda: attn_hi(it, g)})
                    halves(PH_GATE, it, g, half_a)
                    sigmoids(it, g)
            act.wait_ge(attn_ready, HEADS)
            act.wait_ge(pool_ready, PT)
            act.dma_start(xT[:, :, :], scratch).then_inc(x_back, 16)
            def merged_hi(m):
                act.wait_ge(merge_sum, m + 1)
                nc.scalar.activation(hT[:, m * GT:(m + 1) * GT, 0:SEQ], y_sum[:, :, :], ACT.Copy).then_inc(merge_hi, 1)

            for n in range(8):
                it, g = n // 4, n % 4
                lag = {2: lambda: merged_hi(n // 2 - 1)} if n % 2 == 0 and n else ()
                head(PH_BR, it + (g == 3), (g + 1) % 4, after=lag)
                halves(PH_BR, it, g, half_a)
            merged_hi(3)
            with act.Fori(0, 2) as it:
                for g in range(2):
                    rest(PH_WO, it, g)
                    head(PH_WO, it + g, 1 - g)
                    halves(PH_WO, it, g, half_a)
                    act.wait_ge(x1_ready, it * 2 + (g + 1))
                    act.wait_ge(ss_ready, it * 2 + (g + 1))
                    nc.scalar.activation(sq_x1[:, :, :], xT[:, bass.ds(it * (2 * GT) + g * GT, GT), :],
                                         ACT.Square).then_inc(sq1_ready, 1)
            act.dma_start(scratch, xT[:, :, :]).then_inc(spilled, 16)
            nc.scalar.activation(root[:, 0:1], eps[:, 0:1], ACT.Sqrt)
            act.wait_ge(ss_mm, 1)
            nc.scalar.activation(rs_x[:, 0, :], bank[0][:, 0:SEQ], ACT.Sqrt, bias=eps[:, 0:1], scale=1.0 / D).then_inc(rt_ready, 1)
            norm_hi(DT, 0, DT, ADA_SH2 * GT, t_x1)
            act.wait_ge(spilled, 16)

            def tap2(it, g):
                act.wait_ge(sum_ready, it * 2 + (PH_UP.group0 + g + 1))
                for ft in range(GT):
                    t = it * GT + (g * FT + ft)
                    dst = conv_a if g == 0 else conv_b_
                    nc.scalar.activation(dst[:, ft:ft + 1, :], up_pad[:, ft:ft + 1, 2:], ACT.Identity,
                                         bias=par[:, bass.ds(t + PC_CONV[3], 1)],
                                         scale=par[:, bass.ds(t + PC_CONV[2], 1)]).then_inc(tap2_ready, 1)

            def silu(it):
                act.wait_ge(taps_ready, it * 2 + 1)
                nc.scalar.activation(conv_a[:, :, :], conv_a[:, :, :], ACT.Silu).then_inc(silu_a, 1)

            def glu_hi(it):
                act.wait_ge(glu_ready, it + 1)
                nc.scalar.activation(actT[:, bass.ds(it * GT, GT), 0:SEQ], conv_b_[:, :, :], ACT.Copy).then_inc(act_hi, 1)

            for c in (4, 5):
                hi_chunk(PH_UP, 0, 0, c)
            with act.Fori(0, 11) as it:
                rest(PH_UP, it, 0, c0=6)
                head(PH_UP, it, 1)
                halves(PH_UP, it, 0, half_b)
                tap2(it, 0)
                rest(PH_UP, it, 1, after={4: lambda: silu(it)})
                head(PH_UP, it + 1, 0)
                halves(PH_UP, it, 1, half_b)
                tap2(it, 1)
                for c in (4, 5):
                    hi_chunk(PH_UP, it + 1, 0, c)
                glu_hi(it)
            act.wait_ge(chunk_used, PH_UP.chunk_end)
            act.dma_start(x2T[:, :, :], scratch).then_inc(x1_back, 16)

            def copy_out(n, G, b):
                act.wait_ge(out_mm, n + 1)
                nc.scalar.activation(out_tok[:, G, 0, :], bank[b][:, :], ACT.Copy).then_inc(out_copied[0], 1)

            def store(n, G):
                for tok in range(2):
                    act.wait_ge(out_copied[tok], n + 1)
                    act.dma_start(out[0, tok * P:(tok + 1) * P, G * COLS:(G + 1) * COLS],
                                  out_tok[:, G, tok, :]).then_inc(stored, 16)

            for it in range(2):
                rest(PH_DOWN, it, 0, c0=4 if it else 6)
                head(PH_DOWN, it, 1)
                halves(PH_DOWN, it, 0, half_b)
                rest(PH_DOWN, it, 1, after={9: lambda: copy_out(it, 2 * it, 0), 12: lambda: store(it, 2 * it)})
                if it == 0:
                    head(PH_DOWN, 1, 0)
                halves(PH_DOWN, it, 1, half_b)
            for n, G, b in ((2, 1, 2), (3, 3, 0)):
                copy_out(n, G, b)
                store(n, G)
            act.wait_ge(stored, 8 * 16)

        @block.vector
        def _(dve):
            step = Tally(dve_step)

            def link(ins):
                step.inc(ins)
                dve.wait_ge(dve_step, step.value())

            def lo_chunk(ph, it, g, c):
                pos = ph.pos(g, "main", c * CHUNK_T // LOAD_T)
                t0, sc = (c % 2) * CHUNK_T, ph.chunk_slot(g, c)
                dve.wait_ge(hi_ready, ph.chunk(it, g, c) + 1)
                nc.vector.tensor_tensor(w_lo[:, sc, :, :], raw[:, ph.slot(it, pos), t0:t0 + CHUNK_T, :],
                                        w_hi[:, sc, :, :].bitcast(F32), ALU.subtract).then_inc(half_used, 1)

            def ada_load(q, slot, landed, sums, used, pair=ada_acc):
                dve.wait_ge(raw_full[slot], landed)
                if q == 0:
                    if sums is not None:
                        dve.wait_ge(ada_sum, sums)
                else:
                    dve.wait_ge(half_used, used)
                for t in range(LOAD_T):
                    k = q * LOAD_T + t
                    w, s, acc = raw[:, slot, t, :], silu_c[:, k:k + 1], pair[:, k % 2, :]
                    if t >= 2:
                        dve.wait_ge(dve_step, step.value() - 1)
                    if k < 2:
                        ins = nc.vector.tensor_scalar(acc, w, s, None, ALU.mult)
                    else:
                        ins = nc.vector.scalar_tensor_tensor(out=acc, in0=w, scalar=s, in1=acc, op0=ALU.mult, op1=ALU.add)
                    if t < LOAD_T - 1:
                        step.inc(ins)
                    else:
                        ins.then_inc(half_used, 2)

            def mod_store(sums, w, b):
                dve.wait_ge(ada_sum, sums)
                nc.vector.tensor_tensor(mod[:, bass.ds(w * GT, GT)], bank[b][:, 0:GT],
                                        par[:, bass.ds(w * GT + PC_BADA, GT)], ALU.add).then_inc(mod_ready, 1)

            def head(ph, it, g, ada=None, after=()):
                for c in range(4):
                    lo_chunk(ph, it, g, c)
                    if c in after:
                        after[c]()
                    if c == 2 and ada:
                        mod_store(*ada)

            def rest(ph, it, g, after=(), c0=4, before=()):
                for kind, n in ph.order(g)[c0 // 2:]:
                    pos = ph.pos(g, kind, n)
                    if kind == "ada":
                        ada_load(n, ph.slot(it, pos), ph.landed(it, pos), ph.ada_before(it, g), ph.used(it, pos, 0))
                        continue
                    for c in (2 * n, 2 * n + 1):
                        if c in before:
                            before[c]()
                        lo_chunk(ph, it, g, c)
                        if c in after:
                            after[c]()

            def sums(ph, it, g, dst, half):
                dve.wait_ge(half_ready, ph.group(it, g) + 1)
                nc.vector.tensor_tensor(dst, psum[:, 4 * (g % 2):4 * (g % 2) + GT, 0:SEQ], half[:, :, :],
                                        ALU.add).then_inc(sum_ready, 1)

            def summed(ph, it, g):
                dve.wait_ge(sum_ready, ph.group(it, g) + 1)

            def gain_scale(gain, scale, t0, n):
                link(nc.vector.scalar_tensor_tensor(out=scale_a[:, bass.ds(t0, n)], in0=mod[:, bass.ds(t0 + scale, n)],
                                                    scalar=1.0, in1=par[:, bass.ds(t0 + gain, n)],
                                                    op0=ALU.add, op1=ALU.mult))

            def norm(first, t0, n, shift, buf):
                def lo(i):
                    dve.wait_ge(h_hi, t0 + (first + i + 1))
                    t = bass.ds(t0 + i, 1)
                    nc.vector.scalar_tensor_tensor(out=hT[:, t, SEQ:], in0=buf[:, i % 2:i % 2 + 1, :],
                                                   scalar=mod[:, bass.ds(t0 + (shift + i), 1)],
                                                   in1=hT[:, t, 0:SEQ].bitcast(F32), op0=ALU.add,
                                                   op1=ALU.subtract).then_inc(h_ready, 1)

                for i in range(n):
                    if i >= 2:
                        dve.wait_ge(h_ready, t0 + (first + i - 1))
                    t = bass.ds(t0 + i, 1)
                    nc.vector.scalar_tensor_tensor(out=buf[:, i % 2:i % 2 + 1, :], in0=xT[:, t, :], scalar=scale_a[:, t],
                                                   in1=rs_x[:, :, :], op0=ALU.mult, op1=ALU.mult).then_inc(t_ready, 1)
                    if i >= 1:
                        lo(i - 1)
                lo(n - 1)
                dve.wait_ge(h_ready, t0 + (first + n))

            def accumulate(it, j):
                for q in range(LOAD_T):
                    ada_load(q, q, it * 32 + 16 * (j + 1), None, it * 16 + 2 * (4 * j + q), (ada_acc, acc_shift)[j])

            def mixer_store(it, j):
                mod_store(it * 2 + (j + 1), it + (ADA_SC1, ADA_SH1)[j], 4 + j)

            def mixer_norm(it, stored):
                dve.wait_ge(mod_ready, stored)
                gain_scale(PC_GMIX, ADA_SC1 * GT, it * GT, GT)
                norm(0, it * GT, GT, ADA_SH1 * GT, t_x)

            dve.wait_ge(silu_ready, 1)
            accumulate(0, 0)
            accumulate(0, 1)
            dve.wait_ge(rt_ready, 1)
            link(nc.vector.reciprocal(rs_x[:, 0, :], rs_x[:, 0, :]))
            mixer_store(0, 0)
            with dve.Fori(1, 4) as it:
                step.enter(it, 2 * 12 + 1, 1)
                accumulate(it, 0)
                mixer_store(it + (-1), 1)
                mixer_norm(it + (-1), it * 2)
                accumulate(it, 1)
                mixer_store(it, 0)
                step.leave(3)
            for c in range(4):
                lo_chunk(PH_U, 0, 0, c)
            mixer_store(3, 1)
            mixer_norm(3, 8)

            dve.wait_ge(par_ready, 2)
            for g in range(2):
                rest(PH_U, 0, g)
                head(PH_U if g == 0 else PH_QK, 0, 1 - g, (PH_U.ada0 + 1, ADA_SC2, 0) if g else None)
                sums(PH_U, 0, g, u_pad[:, g * GT:(g + 1) * GT, PAD:], half_a)

            def broadcast(a, n):
                return a[:, None, :].to_broadcast([P, n, a.shape[1]])

            def turned(g):
                nc.vector.tensor_tensor(rb[:, :, :], psum[:, 4 * (1 - g):4 * (1 - g) + GT, 0:SEQ],
                                        broadcast(rope_c[:, SEQ:2 * SEQ], GT), ALU.mult).then_inc(rope_sin, 1)

            def turned_q(it):
                dve.wait_ge(d_ready, 1)
                dve.wait_ge(rope_root, it + 1)
                nc.vector.reciprocal(rsq[:, bass.ds(it * (2 * GT), 2 * GT)], root[:, :])
                turned(1)

            with dve.Fori(0, 2) as it:
                step.enter(it, 12)
                for g in range(2):
                    rest(PH_QK, it, g, after={5: lambda: turned_q(it)} if g else ())
                    head(PH_QK, it + g, 1 - g, (it + PH_QK.ada0 + 1, it + (ADA_SC2 + 1), 0) if g else None)
                    sums(PH_QK, it, g, qk[:, bass.ds(it * GT, GT), g, :], half_a)
                dve.wait_ge(rope_out, it + 1)
                step.leave(2)

            def turned_k(g):
                dve.wait_ge(rope_root, 3 + g)
                link(nc.vector.reciprocal(rsk[:, :], root[:, :]))
                nc.vector.tensor_tensor(diag[:, :, :], broadcast(ident, 2 * GT),
                                        rsk[:, :, None].to_broadcast([P, 2 * GT, P]), ALU.mult)
                turned(g)

            def keys(g):
                dve.wait_ge(k_mm, g + 1)
                dve.wait_ge(rope_out, 3 + g)
                k = qk[:, g * GT:(g + 1) * GT, 1, :]
                b0 = 4 * (1 - g)
                scale = psum[:, b0:b0 + 2, :].rearrange("p b n -> p (b n)").rearrange("p (t n) -> p t n", n=SEQ)
                nc.vector.tensor_tensor(k, scale, k, ALU.mult).then_inc(k_ready, 1)

            for g in range(2):
                rest(PH_V, 0, g, after={4: lambda: turned_k(g)})
                head(PH_V if g == 0 else PH_GATE, 0, 1 - g, (PH_V.ada0 + 1, ADA_SC2 + 3, 2) if g else None,
                     after={1: lambda: keys(g)})
                dve.wait_ge(half_ready, PH_V.group(0, g) + 1)
                nc.vector.tensor_copy(v_tok[:, 1, g * COLS:(g + 1) * COLS], bank[4 * g + 1][:, :]).then_inc(sum_ready, 1)

            def maxima(it, g):
                dve.wait_ge(s_mm, it * 2 + (g + 1))
                b, pr, st = bank[4 * (1 - g)], probs[:, g, :], stat[:, g, :]
                for n, (lo, hi) in enumerate(((0, P), (P, QW))):
                    ins = nc.vector.scalar_tensor_tensor(out=pr[:, lo:hi], in0=b[:, lo:hi],
                                                         scalar=rsq[:, bass.ds(it * 4 + (2 * g + n), 1)],
                                                         in1=mask[:, lo:hi], op0=ALU.mult, op1=ALU.add)
                link(ins)
                nc.vector.reduce_max(st[:, 0:1], pr[:, 0:P], AX.X)
                link(nc.vector.reduce_max(st[:, 1:2], pr[:, P:QW], AX.X))
                nc.vector.tensor_scalar(st[:, 2:4], st[:, 0:2], -SCALE, None, ALU.mult).then_inc(max_ready, 1)

            def normalise(it, g):
                dve.wait_ge(exp_ready, it * 2 + (g + 1))
                pr, st = probs[:, g, :], stat[:, g, :]
                link(nc.vector.reciprocal(st[:, 6:8], st[:, 4:6]))
                nc.vector.tensor_scalar(pr[:, 0:P], pr[:, 0:P], st[:, 6:7], None, ALU.mult)
                nc.vector.tensor_scalar(pr[:, P:QW], pr[:, P:QW], st[:, 7:8], None, ALU.mult).then_inc(probs_ready, 1)

            def pool_lo(it, g):
                dve.wait_ge(mix_hi, it * 2 + (g + 1))
                o, b = it * 2 + g, 4 * (1 - g) + 3
                nc.vector.scalar_tensor_tensor(out=poolT[:, bass.ds(o, 1), SEQ:], in0=psum[:, b:b + 1, 0:SEQ],
                                               scalar=par[:, bass.ds(o + PC_PSCALE, 1)],
                                               in1=poolT[:, bass.ds(o, 1), 0:SEQ].bitcast(F32), op0=ALU.mult,
                                               op1=ALU.subtract).then_inc(pool_ready, 1)

            def attn_lo(it, g):
                dve.wait_ge(o_hi, it * 2 + (g + 1))
                h, b = it * 2 + g, 4 * (1 - g) + 2
                nc.vector.tensor_tensor(attnT[:, bass.ds(h, 1), SEQ:], psum[:, b:b + 1, 0:SEQ],
                                        attnT[:, bass.ds(h, 1), 0:SEQ].bitcast(F32), ALU.subtract).then_inc(attn_ready, 1)

            with dve.Fori(0, 4) as it:
                step.enter(it, 12 + 2 * 3)
                for g in range(2):
                    rest(PH_GATE, it, g, after={5: lambda: maxima(it, g), 7: lambda: pool_lo(it, g)},
                         before={6: lambda: normalise(it, g)})
                    head(PH_GATE, it + g, 1 - g, (it + (PH_GATE.ada0 + 1), it + ADA_SH2, 0) if g else None,
                         after={2: lambda: attn_lo(it, g)})
                    sums(PH_GATE, it, g, gates[:, bass.ds(it * GT + g * DT, GT), :], half_a)
                step.leave(4)

            def merged_lo(m):
                dve.wait_ge(merge_hi, m + 1)
                t = slice(m * GT, (m + 1) * GT)
                nc.vector.tensor_tensor(hT[:, t, SEQ:], y_sum[:, :, :], hT[:, t, 0:SEQ].bitcast(F32),
                                        ALU.subtract).then_inc(merged_ready, 1)

            dve.wait_ge(gate_ready, 2 * DT)
            for n in range(8):
                it, g = n // 4, n % 4
                rest(PH_BR, it, g)
                lag = {3: lambda: merged_lo(n // 2 - 1)} if n % 2 == 0 and n else ()
                store = (PH_BR.ada0 + it + 1, ADA_G1 + it, 0) if g == 3 else None
                head(PH_BR, it + (g == 3), (g + 1) % 4, store, after=lag)
                if n >= 3 and n % 2:
                    dve.wait_ge(merged_ready, n // 2)
                sums(PH_BR, it, g, (y_attn, y_sum)[g % 2][:, :, :], half_a)
            merged_lo(3)
            dve.wait_ge(merged_ready, 4)
            dve.wait_ge(x_back, 16)
            with dve.Fori(0, 2) as it:
                step.enter(it, 12)
                for g in range(2):
                    rest(PH_WO, it, g)
                    head(PH_WO, it + g, 1 - g, (it + (PH_WO.ada0 + 1), it + (ADA_G1 + 2), 0) if g else None)
                    sums(PH_WO, it, g, y_sum[:, :, :], half_a)
                    summed(PH_WO, it, g)
                    if g:
                        dve.wait_ge(mod_ready, it + (PH_WO.ada0 + 1))
                    for ft in range(GT):
                        t = it * (2 * GT) + (g * GT + ft)
                        ins = nc.vector.scalar_tensor_tensor(
                            out=xT[:, bass.ds(t, 1), :], in0=y_sum[:, ft:ft + 1, :], scalar=mod[:, bass.ds(t + ADA_G1 * GT, 1)],
                            in1=xT[:, bass.ds(t, 1), :], op0=ALU.mult, op1=ALU.add)
                    ins.then_inc(x1_ready, 1)
                step.leave(2)
            dve.wait_ge(mod_ready, ADA_G2)
            gain_scale(PC_GFFN, ADA_SC2 * GT, 0, DT)
            dve.wait_ge(rt_ready, 2)
            link(nc.vector.reciprocal(rs_x[:, 0, :], rs_x[:, 0, :]))
            norm(DT, 0, DT, ADA_SH2 * GT, t_x1)

            dve.wait_ge(spilled, 16)
            link(nc.vector.memset(up_pad[:, :, 0:2], 0.0))

            def taps(it, g):
                dst = conv_a if g == 0 else conv_b_

                def tap(ft, j):
                    w = par[:, bass.ds(it * GT + (PC_CONV[j] + g * FT + ft), 1)]
                    return nc.vector.scalar_tensor_tensor(out=dst[:, ft, :], in0=up_pad[:, ft, j:j + SEQ], scalar=w,
                                                          in1=dst[:, ft, :], op0=ALU.mult, op1=ALU.add)

                for ft in range(GT):
                    dve.wait_ge(tap2_ready, it * (2 * GT) + (g * GT + ft + 1))
                    step.inc(tap(ft, 1))
                for ft in range(GT):
                    dve.wait_ge(dve_step, step.value() - (GT - 1 - ft))
                    last = tap(ft, 0)
                last.then_inc(taps_ready, 1)
                dve.wait_ge(taps_ready, it * 2 + (g + 1))

            def glu(it):
                dve.wait_ge(silu_a, it + 1)
                nc.vector.tensor_tensor(conv_b_[:, :, :], conv_b_[:, :, :], conv_a[:, :, :], ALU.mult).then_inc(glu_ready, 1)

            def glu_lo(it):
                dve.wait_ge(act_hi, it + 1)
                t = bass.ds(it * GT, GT)
                nc.vector.tensor_tensor(actT[:, t, SEQ:], conv_b_[:, :, :], actT[:, t, 0:SEQ].bitcast(F32),
                                        ALU.subtract).then_inc(act_ready, 1)
                dve.wait_ge(act_ready, it + 1)

            for c in (4, 5):
                lo_chunk(PH_UP, 0, 0, c)
            with dve.Fori(0, 11) as it:
                step.enter(it, 2 * GT)
                for g in range(2):
                    rest(PH_UP, it, g, c0=4 if g else 6)
                    head(PH_UP, it + g, 1 - g)
                    sums(PH_UP, it, g, up_pad[:, :, 2:], half_b)
                    taps(it, g)
                for c in (4, 5):
                    lo_chunk(PH_UP, it + 1, 0, c)
                glu(it)
                glu_lo(it)
                step.leave(11)

            def copy_out(n, G, b):
                dve.wait_ge(out_mm, n + 1)
                nc.vector.tensor_copy(out_tok[:, G, 1, :], bank[b + 1][:, :]).then_inc(out_copied[1], 1)

            for it in range(2):
                for g in range(2):
                    G = 2 * it + g
                    rest(PH_DOWN, it, g, after={9: lambda: copy_out(it, 2 * it, 0)} if g else (), c0=4 if G else 6)
                    store = (PH_DOWN.ada0 + G + 1, ADA_G2 + G, 4 * (1 - g))
                    if G < 3:
                        head(PH_DOWN, it + g, 1 - g, store)
                    else:
                        mod_store(*store)
                    sums(PH_DOWN, it, g, conv_a[:, :, :], half_b)
                    summed(PH_DOWN, it, g)
                    dve.wait_ge(mod_ready, PH_DOWN.ada0 + G + 1)
                    dve.wait_ge(x1_back, 16)
                    for ft in range(GT):
                        t = G * GT + ft
                        dst = x2T[:, t, :] if g else x2_even[:, ft, :]
                        nc.vector.scalar_tensor_tensor(
                            out=dst, in0=conv_a[:, ft, :], scalar=mod[:, ADA_G2 * GT + t:ADA_G2 * GT + t + 1],
                            in1=x2T[:, t, :], op0=ALU.mult, op1=ALU.add).then_inc(x2_ready, 1)
                    dve.wait_ge(x2_ready, (G + 1) * GT)
            for n, G, b in ((2, 1, 2), (3, 3, 0)):
                copy_out(n, G, b)

        @block.tensor
        def _(pe):
            def main_chunk(ph, it, g, c, x, value=False):
                n_chunks, sc = ph.chunks, ph.chunk_slot(g, c)
                pos = ph.pos(g, "main", c * CHUNK_T // LOAD_T)
                pe.wait_ge(half_used, ph.used(it, pos, c % 2 + 1))
                for t in range(CHUNK_T):
                    k = c * CHUNK_T + t
                    first, final = k == 0, k == n_chunks * CHUNK_T - 1
                    if value:
                        for tok in range(2):
                            b = bank[4 * (g % 2) + tok]
                            hi, lo = (x[:, k, o + tok * P:o + (tok + 1) * P] for o in (0, SEQ))
                            nc.tensor.matmul(b[:, :], hi, w_hi[:, sc, t, :], start=first, stop=False)
                            nc.tensor.matmul(b[:, :], hi, w_lo[:, sc, t, :], start=False, stop=False)
                            last = nc.tensor.matmul(b[:, :], lo, w_hi[:, sc, t, :], start=False, stop=final)
                        continue
                    for ft in range(GT):
                        b = bank[4 * (g % 2) + ft]
                        hi, lo = (w[:, sc, t, ft * P:(ft + 1) * P] for w in (w_hi, w_lo))
                        if t == 0:
                            nc.tensor.matmul(b[:, :], hi, x[:, k, :], start=first, stop=False)
                            last = nc.tensor.matmul(b[:, 0:SEQ], lo, x[:, k, 0:SEQ], start=False, stop=False)
                        else:
                            nc.tensor.matmul(b[:, 0:SEQ], lo, x[:, k, 0:SEQ], start=False, stop=False)
                            last = nc.tensor.matmul(b[:, :], hi, x[:, k, :], start=False, stop=final)
                last.then_inc(chunk_used, 1)

            def ada_reduce(b, acc=ada_acc):
                for ft in range(GT):
                    for n in range(2):
                        last = nc.tensor.matmul(bank[b][:, ft:ft + 1], acc[:, n, ft * P:(ft + 1) * P], ones[:, 0:1],
                                                start=n == 0, stop=n == 1)
                last.then_inc(ada_sum, 1)

            def group(ph, it, g, x, value=False, ready=None, between=(), ada_bank=0):
                if ph is not PH_U:
                    pe.wait_ge(sum_ready, ph.group(it, g - 1))
                if not (ph is PH_U and g == 0):
                    pe.wait_ge(mod_ready, ph.ada_before(it, g))
                n_chunks = ph.chunks
                for c in range(n_chunks):
                    if ready:
                        ready(c)
                    if c in between:
                        pe.wait_ge(sum_ready, ph.group(it, g))
                        between[c]()
                    if c == n_chunks - 1 and ph.reduces(g):
                        pe.wait_ge(half_used, ph.used(it, ph.pos(g, "ada", 3), 2))
                        pe.wait_ge(sum_ready, ph.group(it, g))
                        ada_reduce(4 * (1 - g % 2) + ada_bank)
                    main_chunk(ph, it, g, c, x, value)

            pe.wait_ge(square_in, 16)
            pe.wait_ge(par_in, 3 * 16)
            nc.tensor.transpose(bank[7][:, 0:P], par_rows[:, 0, :], ident).then_inc(par_mm, 1)
            pe.wait_ge(x_in, 16)
            for b in range(8):
                if b == 7:
                    pe.wait_ge(par_ready, 1)
                for n in range(4):
                    t, tok = 2 * b + n // 2, n % 2
                    last = nc.tensor.transpose(bank[b][:, n * P:(n + 1) * P], x_tok[:, tok, t * P:(t + 1) * P], ident)
                last.then_inc(xt_mm, 1)
            for b in range(8):
                pe.wait_ge(sqx_ready, b + 1)
                for n in range(2):
                    last = nc.tensor.matmul(bank[0][:, 0:SEQ], ones, sq_x[:, b % 2, n * SEQ:(n + 1) * SEQ],
                                            start=b + n == 0, stop=b + n == 8)
                last.then_inc(sqx_used, 1)
            pe.wait_ge(par_in2, 9 * 16)
            for n in range(1, 6):
                r = PBLOCK_ROWS[n]
                b, o = (bank[1], (n - 1) * P) if n < 5 else (bank[2], 0)
                last = nc.tensor.transpose(b[:, o:o + r], par_rows[0:r, n, :], ident[0:r, 0:r])
            last.then_inc(par_mm, 1)

            def mixer_sums(it, first=False):
                for j, acc in enumerate((ada_acc, acc_shift)):
                    pe.wait_ge(half_used, it * 16 + 8 * (j + 1))
                    if not first:
                        pe.wait_ge(mod_ready, it * 2 + (j - 1))
                    ada_reduce(4 + j, acc)

            mixer_sums(0, True)
            with pe.Fori(1, 4) as it:
                mixer_sums(it)
            pe.wait_ge(par_ready, 2)

            def turn(r, g):
                pe.wait_ge(rope_in, r + 1)
                b0 = 4 * (1 - g)
                for ft in range(GT):
                    nc.tensor.matmul(bank[b0 + ft][:, 0:SEQ], rope_c[:, 2 * SEQ:], tg[:, ft, :], start=True, stop=True)
                for ft in range(GT):
                    for tok in range(2):
                        n = SEQ + 2 * ft + tok
                        last = nc.tensor.matmul(bank[b0][:, n:n + 1], sq[:, ft, tok * P:(tok + 1) * P], ones[:, 0:1],
                                                start=True, stop=True)
                last.then_inc(rope_mm, 1)

            def key_scale(r, g):
                pe.wait_ge(rope_sin, r + 1)
                b0 = 4 * (1 - g)
                for n in range(2):
                    last = nc.tensor.matmul(bank[b0 + n][:, :], ones, diag[:, n * GT:(n + 1) * GT, :], start=True, stop=True)
                last.then_inc(k_mm, 1)

            group(PH_U, 0, 0, hT, ready=lambda c: pe.wait_ge(h_ready, (c + 1) * CHUNK_T))
            group(PH_U, 0, 1, hT)
            pe.wait_ge(const_in, 48)
            with pe.Fori(0, 2) as it:
                group(PH_QK, it, 0, hT)
                group(PH_QK, it, 1, hT, between={4: lambda: turn(it, 1)})
                pe.wait_ge(rope_sin, it + 1)
            for g in range(2):
                group(PH_V, 0, g, hT, value=True, ada_bank=2,
                      between={2: lambda: turn(2 + g, g), 5: lambda: key_scale(2 + g, g)})
                pe.wait_ge(k_ready, g + 1)

            def scores(it, g):
                pe.wait_ge(stage_ready, it * 2 + (g + 1))
                b = bank[4 * (1 - g)]
                k = qk[:, bass.ds(it * 2 + g, 1), 1, :].rearrange("p a n -> p (a n)")
                nc.tensor.matmul(b[:, 0:P], q_st[:, g, 0:P], k[:, 0:P], start=True, stop=True)
                nc.tensor.matmul(b[:, P:QW], q_st[:, g, P:SEQ], k, start=True, stop=True).then_inc(s_mm, 1)

            def turn_probs(it, g):
                pe.wait_ge(probs_ready, it * 2 + (g + 1))
                for n in range(3):
                    last = nc.tensor.transpose(bank[4 * (1 - g) + 1][:, n * P:(n + 1) * P],
                                               probs[:, g, n * P:(n + 1) * P], ident)
                last.then_inc(pt_mm, 1)

            def output(it, g):
                pe.wait_ge(pt_ready, it * 2 + (g + 1))
                b = bank[4 * (1 - g) + 2]
                nc.tensor.matmul(b[:, 0:SEQ], v_st[:, g, 0, :], probsT[:, g, 0:SEQ], start=True, stop=False)
                nc.tensor.matmul(b[:, P:SEQ], v_st[:, g, 1, :], probsT[:, g, SEQ:QW], start=False,
                                 stop=True).then_inc(o_mm, 1)

            def mix(it, g):
                pe.wait_ge(wp_in[g], it * 16 + 16)
                for t in range(2):
                    u = u_pad[:, bass.ds(it * 2 + t, 1), PAD:].rearrange("p a n -> p (a n)")
                    last = nc.tensor.matmul(bank[4 * (1 - g) + 3][:, 0:SEQ], wp_st[:, g, t, :], u,
                                            start=t == 0, stop=t == 1)
                last.then_inc(mix_mm, 1)

            pe.wait_ge(d_ready, 1)
            with pe.Fori(0, 4) as it:
                for g in range(2):
                    group(PH_GATE, it, g, hT, between={2: lambda: scores(it, g), 4: lambda: mix(it, g),
                                                      6: lambda: turn_probs(it, g), 7: lambda: output(it, g)})
                    pe.wait_ge(pool_ready, it * 2 + (g + 1))
                    pe.wait_ge(attn_ready, it * 2 + (g + 1))
            with pe.Fori(0, 2) as it:
                for g in range(4):
                    group(PH_BR, it, g, poolT if g % 2 else attnT)
            with pe.Fori(0, 2) as it:
                group(PH_WO, it, 0, hT,
                      ready=lambda c: pe.wait_ge(merged_ready, 3 if c < 6 else 4) if c in (0, 6) else None)
                group(PH_WO, it, 1, hT)
            pe.wait_ge(ss_ready, 4)
            pe.wait_ge(mod_ready, PH_WO.ada_end)
            for n, squares in enumerate((ss_x1, sq_x1)):
                if n:
                    pe.wait_ge(sq1_ready, 4)
                for ft in range(GT):
                    last = nc.tensor.matmul(bank[0][:, 0:SEQ], ones, squares[:, ft, :], start=n + ft == 0,
                                            stop=n + ft == GT)
            last.then_inc(ss_mm, 1)

            def result(tiles, b0):
                for tok in range(2):
                    for ft in range(GT):
                        last = nc.tensor.transpose(bank[b0 + tok][:, ft * P:(ft + 1) * P],
                                                   tiles[:, ft, tok * P:(tok + 1) * P], ident)
                last.then_inc(out_mm, 1)

            def even_result(it):
                pe.wait_ge(x2_ready, it * (2 * GT) + GT)
                result(x2_even, 0)

            with pe.Fori(0, 11) as it:
                group(PH_UP, it, 0, hT, ready=lambda c: pe.wait_ge(h_ready, DT + (c + 1) * CHUNK_T))
                group(PH_UP, it, 1, hT)
            with pe.Fori(0, 2) as it:
                group(PH_DOWN, it, 0, actT,
                      ready=lambda c: pe.wait_ge(act_ready, 10 if c < 20 else 11) if c in (0, 20) else None)
                group(PH_DOWN, it, 1, actT, between={8: lambda: even_result(it)})
                for n in range(2):
                    pe.wait_ge(out_copied[n], it + 1)
            result(x2T[:, GT:2 * GT, :], 2)
            pe.wait_ge(x2_ready, 4 * GT)
            result(x2T[:, 3 * GT:, :], 0)


_INS = ["x", "c", "w_ada", "b_ada", "norm_mix_g", "w_in", "q_norm_g", "k_norm_g", "w_pool_grp", "pool_scale",
        "w_attn_br", "w_pool_br", "w_gate", "b_gate", "w_o", "norm_ffn_g", "w_up", "conv_w", "conv_b", "w_down"]


def shape_constants():
    square = np.stack([np.eye(P, dtype=np.float32), np.ones((P, P), np.float32)], 1)
    half = HD // 2
    inv = np.float32(10000.0) ** (-np.arange(half, dtype=np.float32) / np.float32(half))
    ang = (np.arange(SEQ, dtype=np.float32)[None, :] * inv.astype(np.float32)[:, None]).astype(np.float32)
    turn = np.zeros((P, P), np.float32)
    turn[np.arange(half) + half, np.arange(half)] = -1.0
    turn[np.arange(half), np.arange(half) + half] = 1.0
    rope = np.concatenate([np.tile(np.cos(ang), (2, 1)), np.tile(np.sin(ang), (2, 1)), turn], 1).astype(np.float32)
    later = np.where(np.arange(P)[None, :] > np.arange(P)[:, None], np.float32(NEG), np.float32(0))
    mask = np.concatenate([later, np.zeros((P, P), np.float32), later], 1).astype(np.float32)
    counts = np.stack([np.minimum(np.arange(SEQ) + 1, w) for w in POOL_WINDOWS])
    invcnt = np.broadcast_to((1.0 / counts).astype(np.float32), (P, 4, SEQ)).copy()
    return {"k_square": square, "k_rope": rope, "k_mask": mask, "k_invcnt": invcnt}


def kernel(**inputs):
    import concourse.bacc as _bacc
    from concourse.bass_utils import run_bass_kernel_spmd as _run

    nc = _bacc.Bacc("TRN2", target_bir_lowering=False, num_devices=1)
    arrays, args = {}, []
    given = {name: np.ascontiguousarray(inputs[name]) for name in _INS}
    given.update(shape_constants())
    for name, a in given.items():
        arrays[f"in_{name}"] = a
        args.append(nc.dram_tensor(f"in_{name}", a.shape, mybir.dt.from_np(a.dtype), kind="ExternalInput").ap())
    args.append(nc.dram_tensor("out", (1, SEQ, D), F32, kind="ExternalOutput").ap())
    args.append(nc.dram_tensor("x1_spill", (P, DT * SEQ), F32, kind="Internal").ap())
    build_block(nc, *args)
    r = _run(nc, [arrays], core_ids=[0])
    return r.results[0]["out"]
```

```python
from contextlib import ExitStack

import concourse.bass as bass
import numpy as np
from concourse import mybir

F32 = mybir.dt.float32
F32R = mybir.dt.float32r
ALU = mybir.AluOpType
ACT = mybir.ActivationFunctionType
AX = mybir.AxisListType

P = 128
SEQ = 256
D = 2048
DT = D // P
HEADS = 8
HD = 128
POOL_WINDOWS = (2, 4, 8, 16)
PT = 1024 // P
FF = 5632
FT = FF // P
EPS = 1e-6
NEG = -1e30
SCALE = float(HD) ** -0.5
COLS = 512
GT = COLS // P
LOAD_T = 4
CHUNK_T = 2
RAW_SLOTS = 4
CHUNK_SLOTS = 4
PAD = max(POOL_WINDOWS)
QW = P + SEQ

FF2T = 2 * FT
PBLOCK_ROWS = [128, 58, FF2T, FF2T, FF2T, FF2T]
PBLOCK_COL = [sum(PBLOCK_ROWS[:n]) for n in range(7)]
PC_C, PC_GMIX, PC_BADA = 0, 16, 32
PC_GFFN, PC_PSCALE, PC_BGATE, PC_QG, PC_KG = 128, 144, 152, 184, 185
PC_CONV = PBLOCK_COL[2:6]

ADA_SH1, ADA_SC1, ADA_G1, ADA_SH2, ADA_SC2, ADA_G2 = 0, 4, 8, 12, 16, 20


class Phase:

    def __init__(self, before, bodies, loads, ada, lead=2, groups=2, held=0):
        self.loads, self.ada, self.lead, self.groups = loads, ada, lead, groups
        self.summed = ada + held
        self.chunks = loads * LOAD_T // CHUNK_T
        self.body_loads = groups * loads + LOAD_T * ada
        self.body_chunks = groups * self.chunks
        self.load0, self.chunk0 = before.load_end, before.chunk_end
        self.group0, self.ada0 = before.group_end, before.ada_end
        self.load_end = self.load0 + bodies * self.body_loads
        self.chunk_end = self.chunk0 + bodies * self.body_chunks
        self.group_end = self.group0 + bodies * groups
        self.ada_end = self.ada0 + bodies * self.summed

    def group(self, it, g):
        return it * self.groups + (self.group0 + g)

    def chunk(self, it, g, c):
        return it * self.body_chunks + (self.chunk0 + g * self.chunks + c)

    def chunk_slot(self, g, c):
        return (g * self.chunks + c) % CHUNK_SLOTS

    def order(self, g):
        seq = [("main", m) for m in range(self.loads)]
        n = self.lead
        if self.ada == 1 and self.groups == 4:
            seq = seq[:2] + [("ada", g)] + seq[2:]
        elif self.ada == 1:
            seq = seq[:n] + [("ada", 2 * g)] + seq[n:n + 1] + [("ada", 2 * g + 1)] + seq[n + 1:]
        if self.ada == 2:
            for a in range(LOAD_T):
                seq.insert(n + 3 * a, ("ada", a))
        return seq

    def pos(self, g, kind, n):
        return self.body_loads // self.groups * g + self.order(g).index((kind, n))

    def ada_before(self, it, g):
        return it * self.summed + (self.ada0 + (g if self.summed == 2 else 0))

    def reduces(self, g):
        return self.summed == 2 or (self.summed == 1 and g == self.groups - 1)

    def load(self, it, pos):
        return it * self.body_loads + (self.load0 + pos)

    def slot(self, it, pos):
        if isinstance(it, int):
            return self.load(it, pos) % RAW_SLOTS
        assert self.load0 % RAW_SLOTS == 0 and self.body_loads % RAW_SLOTS == 0
        return pos % RAW_SLOTS

    def landed(self, it, pos):
        if isinstance(it, int):
            return 16 * (self.load(it, pos) // RAW_SLOTS + 1)
        return it * (16 * self.body_loads // RAW_SLOTS) + 16 * ((self.load0 + pos) // RAW_SLOTS + 1)

    def used(self, it, pos, half):
        return it * (2 * self.body_loads) + (2 * (self.load0 + pos) + half)


class Start:

    def __init__(self):
        seq = []
        for n in range(GT):
            seq += [("pair", n, j, q) for j in range(2) for q in range(LOAD_T)]
            if n:
                seq += [("u", n - 1, g) for g in range(2)]
        seq += [("sc2", 0), ("sc2", 1), ("u", GT - 1, 0), ("u", GT - 1, 1), ("sc2", 2), ("sc2", 3)]
        self.seq = seq
        self.load_end, self.group_end, self.ada_end = len(seq), 2, 2 * GT
        self.chunk_end = self.group_end * DT // CHUNK_T

    def chunks_used(self, g):
        return self.chunk_end - (1 - g) * LOAD_T // CHUNK_T

    def load(self, *key):
        return self.seq.index(key)

    def slot(self, *key):
        return self.load(*key) % RAW_SLOTS

    def landed(self, *key):
        return 16 * (self.load(*key) // RAW_SLOTS + 1)

    def used(self, half, *key):
        return 2 * self.load(*key) + half


START = Start()
PH_QK = Phase(START, 2, 4, 1)
PH_V = Phase(PH_QK, 1, 4, 1, held=1)
PH_GATE = Phase(PH_V, 4, 4, 1)
PH_BR = Phase(PH_GATE, 2, 2, 1, groups=4)
PH_WO = Phase(PH_BR, 2, 4, 1, lead=3)
PH_UP = Phase(PH_WO, 11, 4, 0)
PH_DOWN = Phase(PH_UP, 2, 11, 2, lead=4)


class Tally:

    def __init__(self, sem):
        self.sem, self.n, self.extra = sem, 0, None

    def inc(self, instruction):
        instruction.then_inc(self.sem, 1)
        self.n += 1

    def value(self):
        return self.n if self.extra is None else self.extra + self.n

    def enter(self, it, per, first=0):
        self.start, self.per = self.n, per
        self.extra = it * per + (-first * per)

    def leave(self, count):
        assert self.n - self.start == self.per, (self.n - self.start, self.per)
        self.n = self.start + count * self.per
        self.extra = None


def build_block(nc, x, c, w_ada, b_ada, norm_mix_g, w_in, q_norm_g, k_norm_g, w_pool_grp,
                pool_scale, w_attn_br, w_pool_br, w_gate, b_gate, w_o, norm_ffn_g, w_up,
                conv_w, conv_b, w_down, k_square, k_rope, k_mask, k_invcnt, out, x1_spill):
    ctx = ExitStack()
    with ctx:
        cursor = [nc.sbuf_base + (-nc.sbuf_base) % 64]

        def at(name, shape, dt, offset):
            return nc.alloc_sbuf_tensor_at(name, shape, dt, offset=offset)

        def keep(name, shape, dt=F32):
            t = at(name, shape, dt, cursor[0])
            cursor[0] += int(np.prod(shape[1:])) * 4
            cursor[0] += (-cursor[0]) % 32
            return t

        def sem(name):
            return ctx.enter_context(nc.semaphore(name))

        raw = keep("raw", [P, RAW_SLOTS, LOAD_T, COLS])
        w_hi = keep("w_hi", [P, CHUNK_SLOTS, CHUNK_T, COLS], F32R)
        w_lo = keep("w_lo", [P, CHUNK_SLOTS, CHUNK_T, COLS], F32R)
        square = keep("square", [P, 2, P])
        par = keep("par", [P, PBLOCK_COL[6]])
        mod = keep("mod", [P, 6 * DT])
        silu_c = keep("silu_c", [P, DT])
        scale_a = keep("scale_a", [P, DT])
        eps = keep("eps", [P, 1])
        ada_acc = keep("ada_acc", [P, 2, COLS])
        rsq = keep("rsq", [P, 2 * HEADS])
        h0 = cursor[0]
        hT = keep("hT", [P, DT, 2 * SEQ], F32R)
        x0 = cursor[0]
        xT = keep("xT", [P, DT, SEQ])
        cursor[0] += 64
        big = cursor[0]
        actT = keep("actT", [P, FT, 2 * SEQ], F32R)
        ident, ones = square[:, 0, :], square[:, 1, :]

        def early(name, shape, offset, dt=F32):
            assert offset + int(np.prod(shape[1:])) * 4 <= FT * 2 * SEQ * 4
            return at(name, shape, dt, big + offset)

        attnT = early("attnT", [P, HEADS, 2 * SEQ], 0, F32R)
        poolT = early("poolT", [P, PT, 2 * SEQ], 16384, F32R)
        gates = early("gates", [P, 2 * DT, SEQ], 32768)
        qk = early("qk", [P, HEADS, 2, SEQ], 49152)
        v_tok = early("v_tok", [P, 2, HEADS * HD], 65536)
        u_pad = early("u_pad", [P, PT, PAD + SEQ], 73728)
        half_a = early("half_a", [P, GT, SEQ], 82432)
        rs_x = early("rs_x", [P, 1, SEQ], 87552)
        mask = early("mask", [P, QW], 88576)
        x_tok = early("x_tok", [P, 2, D], 0)
        par_rows = early("par_rows", [P, 6, P], 16384)
        sq_x = early("sq_x", [P, 2, 2 * SEQ], 20480)
        t_x = early("t_x", [P, 2, SEQ], 26624)
        acc_shift = early("acc_shift", [P, 2, COLS], 45056)
        pool_s = [early(f"pool_s{n}", [P, PT, PAD + SEQ], n * 8704) for n in range(2)]
        tg = early("tg", [P, GT, SEQ], 17408)
        sq = early("sq", [P, GT, SEQ], 21504)
        rb = early("rb", [P, GT, SEQ], 25600)
        diag = early("diag", [P, 2 * GT, P], 29696)
        root = early("root", [P, 2 * GT], 33792)
        rsk = early("rsk", [P, 2 * GT], 33824)
        rope_c = early("rope_c", [P, 2 * SEQ + P], 36864)
        invcnt = early("invcnt", [P, 4, SEQ], 40960)
        probs = at("probs", [P, 2, QW], F32, x0)
        probsT = at("probsT", [P, 2, QW], F32, x0 + 3072)
        q_st = at("q_st", [P, 2, SEQ], F32, x0 + 6144)
        v_st = at("v_st", [P, 2, 2, HD], F32, x0 + 8192)
        wp_st = at("wp_st", [P, 2, 2, P], F32, x0 + 10240)
        stat = at("stat", [P, 2, 8], F32, x0 + 12288)
        y_attn = early("y_attn", [P, GT, SEQ], 65536)
        y_sum = early("y_sum", [P, GT, SEQ], 69632)
        sq_x1 = early("sq_x1", [P, GT, SEQ], 0)
        ss_x1 = early("ss_x1", [P, GT, SEQ], 4096)
        t_x1 = early("t_x1", [P, 2, SEQ], 8192)
        half_b = at("half_b", [P, GT, SEQ], F32, x0)
        up_pad = at("up_pad", [P, GT, 2 + SEQ], F32, x0 + 4096)
        conv_a = at("conv_a", [P, GT, SEQ], F32, x0 + 4096 + 4128)
        conv_b_ = at("conv_bb", [P, GT, SEQ], F32, x0 + 8192 + 4128)
        x2T = at("x2T", [P, DT, SEQ], F32, h0)
        x2_even = conv_b_
        out_tok = at("out_tok", [P, 4, 2, COLS], F32, h0 + 16384)

        psum = ctx.enter_context(nc.psum_tensor("psum", [P, 8, 512], F32))
        bank = [psum[:, n, :] for n in range(8)]

        x_in, par_in, square_in, const_in = sem("x_in"), sem("par_in"), sem("square_in"), sem("const_in")
        par_in2 = sem("par_in2")
        raw_full = [sem(f"raw_full{n}") for n in range(RAW_SLOTS)]
        half_used = sem("half_used")
        hi_ready = sem("hi_ready")
        chunk_used = sem("chunk_used")
        half_ready = sem("half_ready")
        sum_ready = sem("sum_ready")
        ada_sum = sem("ada_sum")
        mod_ready = sem("mod_ready")
        dve_step = sem("dve_step")
        pool_step = sem("pool_step")
        xt_mm, xt_ready = sem("xt_mm"), sem("xt_ready")
        par_mm, par_ready = sem("par_mm"), sem("par_ready")
        silu_ready = sem("silu_ready")
        eps_ready = sem("eps_ready")
        sqx_ready, sqx_used = sem("sqx_ready"), sem("sqx_used")
        ss_ready, ss_mm, rt_ready = sem("ss_ready"), sem("ss_mm"), sem("rt_ready")
        t_ready, h_hi, h_ready = sem("t_ready"), sem("h_hi"), sem("h_ready")
        d_ready = sem("d_ready")
        rope_in = sem("rope_in")
        rope_mm = sem("rope_mm")
        rope_root = sem("rope_root")
        rope_sin = sem("rope_sin")
        rope_out = sem("rope_out")
        k_mm, k_ready = sem("k_mm"), sem("k_ready")
        stage_ready = sem("stage_ready")
        wp_in = [sem(f"wp_in{n}") for n in range(2)]
        s_mm, max_ready, exp_ready, probs_ready = sem("s_mm"), sem("max_ready"), sem("exp_ready"), sem("probs_ready")
        pt_mm, pt_ready, o_mm, o_hi, attn_ready = sem("pt_mm"), sem("pt_ready"), sem("o_mm"), sem("o_hi"), sem("attn_ready")
        mix_mm, mix_hi, pool_ready = sem("mix_mm"), sem("mix_hi"), sem("pool_ready")
        gate_ready = sem("gate_ready")
        merge_sum, merge_hi, merged_ready = sem("merge_sum"), sem("merge_hi"), sem("merged_ready")
        x1_ready, sq1_ready = sem("x1_ready"), sem("sq1_ready")
        tap2_ready, taps_ready, silu_a = sem("tap2_ready"), sem("taps_ready"), sem("silu_a")
        glu_ready, act_hi, act_ready = sem("glu_ready"), sem("act_hi"), sem("act_ready")
        x_spilled, x_back, spilled, x1_back = sem("x_spilled"), sem("x_back"), sem("spilled"), sem("x1_back")
        x2_ready, out_mm, stored = sem("x2_ready"), sem("out_mm"), sem("stored")
        out_copied = [sem(f"out_copied{n}") for n in range(2)]

        def tiles(w):
            return w.rearrange("(t p) n -> p t n", p=P)

        def rows(w, t0, col):
            return tiles(w)[:, t0:t0 + LOAD_T, bass.ds(col, COLS)]

        def flat(w):
            return w.rearrange("(t p) -> t p", p=P)

        block = ctx.enter_context(nc.Block())

        @block.sync
        def _(sp):
            def load(src, it, ph, pos):
                slot = ph.slot(it, pos)
                sp.wait_ge(half_used, ph.used(it, pos - RAW_SLOTS, 2))
                sp.dma_start(raw[:, slot, :, :], src).then_inc(raw_full[slot], 16)

            def body(ph, it, mains, adas):
                pos = 0
                for g in range(ph.groups):
                    for kind, n in ph.order(g):
                        w, col = mains[g] if kind == "main" else (w_ada[0], adas[g % len(adas)] * COLS)
                        load(rows(w, n * LOAD_T, col), it, ph, pos)
                        pos += 1

            sp.dma_start(square[:, :, :], k_square).then_inc(square_in, 16)
            for r0, blk, src in ((0, 0, flat(c[0])), (16, 0, flat(norm_mix_g[0])), (32, 0, flat(b_ada[0]))):
                sp.dma_start(par_rows[r0:r0 + src.shape[0], blk, :], src).then_inc(par_in, 16)
            for n, key in enumerate(START.seq):
                if key[0] == "pair":
                    w = (ADA_SC1, ADA_SH1)[key[2]] + key[1]
                    src = rows(w_ada[0], key[3] * LOAD_T, w * COLS)
                elif key[0] == "u":
                    src = rows(w_in[0], key[1] * LOAD_T, 3072 + key[2] * COLS)
                else:
                    src = rows(w_ada[0], key[1] * LOAD_T, ADA_SC2 * COLS)
                if n >= RAW_SLOTS:
                    sp.wait_ge(half_used, 2 * (n - RAW_SLOTS + 1))
                sp.dma_start(raw[:, n % RAW_SLOTS, :, :], src).then_inc(raw_full[n % RAW_SLOTS], 16)
                if n == 20:
                    sp.dma_start(rope_c[:, :], k_rope).then_inc(const_in, 16)
                    sp.dma_start(mask[:, :], k_mask).then_inc(const_in, 16)
                    sp.dma_start(invcnt[:, :, :], k_invcnt).then_inc(const_in, 16)
            with sp.Fori(0, 2) as it:
                body(PH_QK, it, [(w_in[0], it * COLS), (w_in[0], it * COLS + 1024)], [it + (ADA_SC2 + 1)])
            body(PH_V, 0, [(w_in[0], 2048), (w_in[0], 2560)], [ADA_SC2 + 3])
            with sp.Fori(0, 4) as it:
                body(PH_GATE, it, [(w_gate[0], it * COLS), (w_gate[0], it * COLS + D)], [it + ADA_SH2])
            with sp.Fori(0, 2) as it:
                body(PH_BR, it, [(w, it * (2 * COLS) + n * COLS) for n in range(2) for w in (w_attn_br[0], w_pool_br[0])],
                     [it + ADA_G1])
            with sp.Fori(0, 2) as it:
                body(PH_WO, it, [(w_o[0], it * (2 * COLS)), (w_o[0], it * (2 * COLS) + COLS)], [it + (ADA_G1 + 2)])
            with sp.Fori(0, 11) as it:
                body(PH_UP, it, [(w_up[0], it * COLS), (w_up[0], it * COLS + FF)], [0])
            for it in range(2):
                body(PH_DOWN, it, [(w_down[0], 2 * it * COLS), (w_down[0], (2 * it + 1) * COLS)],
                     [ADA_G2 + 2 * it, ADA_G2 + 2 * it + 1])

        @block.gpsimd
        def _(pool):
            step = Tally(pool_step)

            def link(ins):
                step.inc(ins)
                pool.wait_ge(pool_step, step.value())

            nc.gpsimd.memset(eps[:, :], EPS).then_inc(eps_ready, 1)
            pool.wait_ge(xt_mm, 8)
            pool.wait_ge(par_mm, 2)
            for t in (u_pad, pool_s[0], pool_s[1]):
                link(nc.gpsimd.memset(t[:, :, 0:PAD], 0.0))
            pool.wait_ge(sum_ready, 2)
            pool.wait_ge(const_in, 48)
            src = u_pad
            for n, w in enumerate(POOL_WINDOWS):
                dst, other, t0 = pool_s[n % 2], pool_s[(n + 1) % 2], 2 * n
                link(nc.gpsimd.tensor_tensor(dst[:, t0:, PAD:], src[:, t0:, PAD:],
                                             src[:, t0:, PAD - w // 2:PAD + SEQ - w // 2], ALU.add))
                for t in (t0, t0 + 1):
                    link(nc.gpsimd.tensor_tensor(other[:, t, PAD:], dst[:, t, PAD:], invcnt[:, n, :], ALU.mult))
                    last = nc.gpsimd.tensor_tensor(u_pad[:, t, PAD:], other[:, t, PAD:], u_pad[:, t, PAD:], ALU.subtract)
                    if n < len(POOL_WINDOWS) - 1 or t == t0:
                        link(last)
                src = dst
            last.then_inc(d_ready, 1)
            pool.wait_ge(d_ready, 1)

            def turn(r, head0, which):
                heads = [qk[:, head0 + ft, which, :] for ft in range(GT)]
                pool.wait_ge(rope_in, r + 1)
                for ft in range(GT):
                    link(nc.gpsimd.tensor_tensor(heads[ft], tg[:, ft, :], rope_c[:, 0:SEQ], ALU.mult))
                pool.wait_ge(rope_sin, r + 1)
                for ft in range(GT):
                    last = nc.gpsimd.tensor_tensor(heads[ft], heads[ft], rb[:, ft, :], ALU.add)
                last.then_inc(rope_out, 1)

            for r, (head0, which) in enumerate(((0, 0), (GT, 0), (0, 1), (GT, 1))):
                turn(r, head0, which)

            def stage(h, g):
                nc.gpsimd.tensor_copy(q_st[:, g:g + 1, :], qk[:, bass.ds(h, 1), 0, :])
                nc.gpsimd.tensor_copy(v_st[:, g, :, :], v_tok[:, :, bass.ds(h * HD, HD)]).then_inc(stage_ready, 1)

            pool.wait_ge(x_spilled, 16)
            pool.wait_ge(rope_out, 4)
            pool.wait_ge(sum_ready, PH_V.group_end)
            for g in range(2):
                stage(g, g)
            with pool.Fori(1, HEADS // 2) as it:
                for g in range(2):
                    pool.wait_ge(o_mm, it * 2 + (g - 1))
                    stage(it * 2 + g, g)

            pool.wait_ge(gate_ready, 2 * DT)
            for m in range(GT):
                for n, y in enumerate((y_attn, y_sum)):
                    pool.wait_ge(sum_ready, PH_BR.group0 + 2 * m + n + 1)
                    t = n * DT + m * GT
                    link(nc.gpsimd.tensor_tensor(y[:, :, :], y[:, :, :], gates[:, t:t + GT, :], ALU.mult))
                nc.gpsimd.tensor_tensor(y_sum[:, :, :], y_sum[:, :, :], y_attn[:, :, :], ALU.add).then_inc(merge_sum, 1)

            pool.wait_ge(chunk_used, PH_BR.chunk_end)
            nc.gpsimd.memset(ss_x1[:, :, :], 0.0).then_inc(ss_ready, 1)
            for G in range(3):
                pool.wait_ge(ss_ready, G + 1)
                pool.wait_ge(sq1_ready, G + 1)
                nc.gpsimd.tensor_tensor(ss_x1[:, :, :], ss_x1[:, :, :], sq_x1[:, :, :], ALU.add).then_inc(ss_ready, 1)

        @block.scalar
        def _(act):
            def hi_chunk(ph, it, g, c):
                pos = ph.pos(g, "main", c * CHUNK_T // LOAD_T)
                act.wait_ge(chunk_used, ph.chunk(it, g, c - CHUNK_SLOTS + 1))
                if c % 2 == 0:
                    act.wait_ge(raw_full[ph.slot(it, pos)], ph.landed(it, pos))
                t0 = (c % 2) * CHUNK_T
                nc.scalar.activation(w_hi[:, ph.chunk_slot(g, c), :, :], raw[:, ph.slot(it, pos), t0:t0 + CHUNK_T, :],
                                     ACT.Copy).then_inc(hi_ready, 1)

            def head(ph, it, g, after=(), chunks=4):
                for c in range(chunks):
                    hi_chunk(ph, it, g, c)
                    if c in after:
                        after[c]()

            def rest(ph, it, g, after=(), c0=4):
                for c in range(c0, ph.loads * 2):
                    hi_chunk(ph, it, g, c)
                    if c in after:
                        after[c]()

            def halves(ph, it, g, half):
                act.wait_ge(chunk_used, ph.chunk(it, g, ph.chunks))
                act.wait_ge(sum_ready, ph.group(it, g))
                nc.scalar.activation(half[:, :, :], psum[:, 4 * (g % 2):4 * (g % 2) + GT, SEQ:],
                                     ACT.Copy).then_inc(half_ready, 1)

            act.dma_start(x_tok[:, :, :], x[0].rearrange("(t p) n -> p t n", p=P)).then_inc(x_in, 16)
            for r0, blk, src in ((0, 1, flat(norm_ffn_g[0])), (16, 1, flat(pool_scale[0])),
                                 (24, 1, flat(b_gate[0])), (56, 1, q_norm_g), (57, 1, k_norm_g),
                                 (0, 2, flat(conv_w[0, 0])), (0, 3, flat(conv_w[0, 1])),
                                 (0, 4, flat(conv_w[0, 2])), (0, 5, flat(conv_b[0]))):
                act.dma_start(par_rows[r0:r0 + src.shape[0], blk, :], src).then_inc(par_in2, 16)
            act.wait_ge(par_mm, 1)
            nc.scalar.activation(par[:, 0:P], bank[7][:, 0:P], ACT.Copy).then_inc(par_ready, 1)
            act.wait_ge(par_ready, 1)
            nc.scalar.activation(silu_c[:, :], par[:, PC_C:PC_C + DT], ACT.Silu).then_inc(silu_ready, 1)
            for b in range(8):
                act.wait_ge(xt_mm, b + 1)
                two = xT[:, 2 * b:2 * b + 2, :].rearrange("p t n -> p (t n)")
                nc.scalar.activation(two, bank[b][:, :], ACT.Copy).then_inc(xt_ready, 1)
                act.wait_ge(xt_ready, b + 1)
                if b >= 2:
                    act.wait_ge(sqx_used, b - 1)
                nc.scalar.activation(sq_x[:, b % 2, :], two, ACT.Square).then_inc(sqx_ready, 1)
            act.wait_ge(sqx_used, 8)
            act.wait_ge(eps_ready, 1)
            nc.scalar.activation(rs_x[:, 0, :], bank[0][:, 0:SEQ], ACT.Sqrt, bias=eps[:, 0:1], scale=1.0 / D).then_inc(rt_ready, 1)
            act.wait_ge(par_mm, 2)
            for n in range(1, 6):
                r = PBLOCK_ROWS[n]
                b, o = (bank[5], (n - 1) * P) if n < 5 else (bank[6], 0)
                last = nc.scalar.activation(par[:, PBLOCK_COL[n]:PBLOCK_COL[n] + r], b[:, o:o + r], ACT.Copy)
            last.then_inc(par_ready, 1)

            def norm_hi(first, t0, n, shift, buf):
                for i in range(n):
                    act.wait_ge(t_ready, t0 + (first + i + 1))
                    nc.scalar.activation(hT[:, bass.ds(t0 + i, 1), 0:SEQ], buf[:, i % 2:i % 2 + 1, :], ACT.Identity,
                                         bias=mod[:, bass.ds(t0 + (shift + i), 1)]).then_inc(h_hi, 1)

            def first_hi(m):
                for k in range(4 * m, 4 * m + 4):
                    g, half = k % 4 // 2, k % 2
                    if m:
                        act.wait_ge(chunk_used, k - CHUNK_SLOTS + 1)
                    if half == 0:
                        act.wait_ge(raw_full[START.slot("u", m, g)], START.landed("u", m, g))
                    nc.scalar.activation(w_hi[:, k % 4, :, :],
                                         raw[:, START.slot("u", m, g), half * CHUNK_T:(half + 1) * CHUNK_T, :],
                                         ACT.Copy).then_inc(hi_ready, 1)

            def u_half(g):
                act.wait_ge(chunk_used, START.chunks_used(g))
                nc.scalar.activation(u_pad[:, g * GT:g * GT + 2, PAD:],
                                     bank[4 + 2 * g].rearrange("p (t n) -> p t n", n=SEQ), ACT.Copy).then_inc(half_ready, 1)

            act.wait_ge(par_ready, 2)
            for m in range(GT):
                norm_hi(0, m * GT, GT, ADA_SH1 * GT, t_x)
                first_hi(m)
            scratch = x1_spill.rearrange("p (t n) -> p t n", n=SEQ)
            act.dma_start(scratch, xT[:, :, :]).then_inc(x_spilled, 16)
            head(PH_QK, 0, 0, after={1: lambda: u_half(0), 3: lambda: u_half(1)})

            def rope_inputs(head0, which, gain):
                four = qk[:, bass.ds(head0, GT), which, :]
                act.wait_ge(d_ready, 1)
                nc.scalar.activation(tg[:, :, :], four, ACT.Copy, scale=par[:, gain:gain + 1])
                nc.scalar.activation(sq[:, :, :], four, ACT.Square).then_inc(rope_in, 1)

            def rope_rms(r, g):
                act.wait_ge(rope_mm, r + 1)
                nc.scalar.activation(root[:, :], bank[4 * (1 - g)][:, SEQ:SEQ + 2 * GT], ACT.Sqrt, bias=eps[:, 0:1],
                                     scale=1.0 / HD).then_inc(rope_root, 1)

            with act.Fori(0, 2) as it:
                rest(PH_QK, it, 0)
                head(PH_QK, it, 1)
                halves(PH_QK, it, 0, half_a)
                act.wait_ge(sum_ready, it * 2 + (PH_QK.group0 + 1))
                rope_inputs(it * GT, 0, PC_QG)
                rest(PH_QK, it, 1, after={5: lambda: rope_rms(it, 1)})
                head(PH_QK, it + 1, 0)
                halves(PH_QK, it, 1, half_a)
                act.wait_ge(rope_out, it + 1)

            def v_half(g):
                act.wait_ge(chunk_used, PH_V.chunk(0, g, PH_V.chunks))
                nc.scalar.activation(v_tok[:, 0, g * COLS:(g + 1) * COLS], bank[4 * g][:, :], ACT.Copy).then_inc(half_ready, 1)

            for g in range(2):
                if g == 0:
                    act.wait_ge(sum_ready, PH_QK.group_end)
                else:
                    act.wait_ge(rope_out, 3)
                rope_inputs(g * GT, 1, PC_KG)
                rest(PH_V, 0, g, after={4: lambda: rope_rms(2 + g, g)})
                head(PH_V if g == 0 else PH_GATE, 0, 1 - g)
                v_half(g)

            def exponentials(it, g):
                act.wait_ge(max_ready, it * 2 + (g + 1))
                nc.scalar.activation(probs[:, g, 0:P], probs[:, g, 0:P], ACT.Exp, bias=stat[:, g, 2:3],
                                     scale=SCALE, accum_out=stat[:, g, 4:5])
                nc.scalar.activation(probs[:, g, P:QW], probs[:, g, P:QW], ACT.Exp, bias=stat[:, g, 3:4],
                                     scale=SCALE, accum_out=stat[:, g, 5:6]).then_inc(exp_ready, 1)

            def pool_hi(it, g):
                act.wait_ge(mix_mm, it * 2 + (g + 1))
                o = it * 2 + g
                nc.scalar.activation(poolT[:, bass.ds(o, 1), 0:SEQ], psum[:, 4 * (1 - g) + 3:4 * (1 - g) + 4, 0:SEQ],
                                     ACT.Copy, scale=par[:, bass.ds(o + PC_PSCALE, 1)]).then_inc(mix_hi, 1)

            def probs_turned(it, g):
                act.wait_ge(pt_mm, it * 2 + (g + 1))
                nc.scalar.activation(probsT[:, g, :], bank[4 * (1 - g) + 1][:, 0:QW], ACT.Copy).then_inc(pt_ready, 1)

            def attn_hi(it, g):
                act.wait_ge(o_mm, it * 2 + (g + 1))
                nc.scalar.activation(attnT[:, bass.ds(it * 2 + g, 1), 0:SEQ],
                                     psum[:, 4 * (1 - g) + 2:4 * (1 - g) + 3, 0:SEQ], ACT.Copy).then_inc(o_hi, 1)

            def sigmoids(it, g):
                act.wait_ge(sum_ready, it * 2 + (PH_GATE.group0 + g + 1))
                for ft in range(GT):
                    t = it * GT + (g * DT + ft)
                    nc.scalar.activation(gates[:, bass.ds(t, 1), :], gates[:, bass.ds(t, 1), :], ACT.Sigmoid,
                                         bias=par[:, bass.ds(t + PC_BGATE, 1)]).then_inc(gate_ready, 1)

            with act.Fori(0, 4) as it:
                for g in range(2):
                    wp = w_pool_grp[0].rearrange("g c n -> (g c) n").rearrange("(t p) n -> p t n", p=P)
                    act.dma_start(wp_st[:, g, :, :], wp[:, bass.ds(it * 2, 2), g * P:(g + 1) * P]).then_inc(wp_in[g], 16)
                    rest(PH_GATE, it, g, after={5: lambda: exponentials(it, g), 6: lambda: pool_hi(it, g)})
                    head(PH_GATE, it + g, 1 - g, after={1: lambda: probs_turned(it, g), 2: lambda: attn_hi(it, g)})
                    halves(PH_GATE, it, g, half_a)
                    sigmoids(it, g)
            act.wait_ge(attn_ready, HEADS)
            act.wait_ge(pool_ready, PT)
            act.dma_start(xT[:, :, :], scratch).then_inc(x_back, 16)
            def merged_hi(m):
                act.wait_ge(merge_sum, m + 1)
                nc.scalar.activation(hT[:, m * GT:(m + 1) * GT, 0:SEQ], y_sum[:, :, :], ACT.Copy).then_inc(merge_hi, 1)

            for n in range(8):
                it, g = n // 4, n % 4
                lag = {2: lambda: merged_hi(n // 2 - 1)} if n % 2 == 0 and n else ()
                head(PH_BR, it + (g == 3), (g + 1) % 4, after=lag)
                halves(PH_BR, it, g, half_a)
            merged_hi(3)
            with act.Fori(0, 2) as it:
                for g in range(2):
                    rest(PH_WO, it, g)
                    head(PH_WO, it + g, 1 - g, chunks=3)
                    halves(PH_WO, it, g, half_a)
                    hi_chunk(PH_WO, it + g, 1 - g, 3)
                    act.wait_ge(x1_ready, it * 2 + (g + 1))
                    act.wait_ge(ss_ready, it * 2 + (g + 1))
                    nc.scalar.activation(sq_x1[:, :, :], xT[:, bass.ds(it * (2 * GT) + g * GT, GT), :],
                                         ACT.Square).then_inc(sq1_ready, 1)
            act.dma_start(scratch, xT[:, :, :]).then_inc(spilled, 16)
            nc.scalar.activation(root[:, 0:1], eps[:, 0:1], ACT.Sqrt)
            act.wait_ge(ss_mm, 1)
            nc.scalar.activation(rs_x[:, 0, :], bank[0][:, 0:SEQ], ACT.Sqrt, bias=eps[:, 0:1], scale=1.0 / D).then_inc(rt_ready, 1)
            norm_hi(DT, 0, DT, ADA_SH2 * GT, t_x1)
            act.wait_ge(spilled, 16)

            def tap2(it, g):
                act.wait_ge(sum_ready, it * 2 + (PH_UP.group0 + g + 1))
                for ft in range(GT):
                    t = it * GT + (g * FT + ft)
                    dst = conv_a if g == 0 else conv_b_
                    nc.scalar.activation(dst[:, ft:ft + 1, :], up_pad[:, ft:ft + 1, 2:], ACT.Identity,
                                         bias=par[:, bass.ds(t + PC_CONV[3], 1)],
                                         scale=par[:, bass.ds(t + PC_CONV[2], 1)]).then_inc(tap2_ready, 1)

            def silu(it):
                act.wait_ge(taps_ready, it * 2 + 1)
                nc.scalar.activation(conv_a[:, :, :], conv_a[:, :, :], ACT.Silu).then_inc(silu_a, 1)

            def glu_hi(it):
                act.wait_ge(glu_ready, it + 1)
                nc.scalar.activation(actT[:, bass.ds(it * GT, GT), 0:SEQ], conv_b_[:, :, :], ACT.Copy).then_inc(act_hi, 1)

            for c in (4, 5, 6):
                hi_chunk(PH_UP, 0, 0, c)
            with act.Fori(0, 11) as it:
                rest(PH_UP, it, 0, c0=7)
                head(PH_UP, it, 1)
                halves(PH_UP, it, 0, half_b)
                tap2(it, 0)
                rest(PH_UP, it, 1, after={4: lambda: silu(it)})
                head(PH_UP, it + 1, 0)
                halves(PH_UP, it, 1, half_b)
                tap2(it, 1)
                for c in (4, 5, 6):
                    hi_chunk(PH_UP, it + 1, 0, c)
                glu_hi(it)
            act.wait_ge(chunk_used, PH_UP.chunk_end)
            act.dma_start(x2T[:, :, :], scratch).then_inc(x1_back, 16)

            def copy_out(n, G, b):
                act.wait_ge(out_mm, n + 1)
                nc.scalar.activation(out_tok[:, G, 0, :], bank[b][:, :], ACT.Copy).then_inc(out_copied[0], 1)

            def store(n, G):
                for tok in range(2):
                    act.wait_ge(out_copied[tok], n + 1)
                    act.dma_start(out[0, tok * P:(tok + 1) * P, G * COLS:(G + 1) * COLS],
                                  out_tok[:, G, tok, :]).then_inc(stored, 16)

            for it in range(2):
                rest(PH_DOWN, it, 0, c0=4 if it else 7)
                head(PH_DOWN, it, 1)
                halves(PH_DOWN, it, 0, half_b)
                rest(PH_DOWN, it, 1, after={9: lambda: copy_out(it, 2 * it, 0), 12: lambda: store(it, 2 * it)})
                if it == 0:
                    head(PH_DOWN, 1, 0)
                halves(PH_DOWN, it, 1, half_b)
            for n, G, b in ((2, 1, 2), (3, 3, 0)):
                copy_out(n, G, b)
                store(n, G)
            act.wait_ge(stored, 8 * 16)

        @block.vector
        def _(dve):
            step = Tally(dve_step)

            def link(ins):
                step.inc(ins)
                dve.wait_ge(dve_step, step.value())

            def lo_chunk(ph, it, g, c):
                pos = ph.pos(g, "main", c * CHUNK_T // LOAD_T)
                t0, sc = (c % 2) * CHUNK_T, ph.chunk_slot(g, c)
                dve.wait_ge(hi_ready, ph.chunk(it, g, c) + 1)
                nc.vector.tensor_tensor(w_lo[:, sc, :, :], raw[:, ph.slot(it, pos), t0:t0 + CHUNK_T, :],
                                        w_hi[:, sc, :, :].bitcast(F32), ALU.subtract).then_inc(half_used, 1)

            def ada_load(q, slot, landed, sums, used, pair=ada_acc):
                dve.wait_ge(raw_full[slot], landed)
                if q == 0:
                    if sums is not None:
                        dve.wait_ge(ada_sum, sums)
                else:
                    dve.wait_ge(half_used, used)
                for t in range(LOAD_T):
                    k = q * LOAD_T + t
                    w, s, acc = raw[:, slot, t, :], silu_c[:, k:k + 1], pair[:, k % 2, :]
                    if t >= 2:
                        dve.wait_ge(dve_step, step.value() - 1)
                    if k < 2:
                        ins = nc.vector.tensor_scalar(acc, w, s, None, ALU.mult)
                    else:
                        ins = nc.vector.scalar_tensor_tensor(out=acc, in0=w, scalar=s, in1=acc, op0=ALU.mult, op1=ALU.add)
                    if t < LOAD_T - 1:
                        step.inc(ins)
                    else:
                        ins.then_inc(half_used, 2)

            def mod_store(sums, w, b):
                dve.wait_ge(ada_sum, sums)
                nc.vector.tensor_tensor(mod[:, bass.ds(w * GT, GT)], bank[b][:, 0:GT],
                                        par[:, bass.ds(w * GT + PC_BADA, GT)], ALU.add).then_inc(mod_ready, 1)

            def head(ph, it, g, ada=None, after=(), chunks=4):
                for c in range(chunks):
                    lo_chunk(ph, it, g, c)
                    if c in after:
                        after[c]()
                    if c == 2 and ada:
                        mod_store(*ada)

            def rest(ph, it, g, after=(), c0=4, before=()):
                for kind, n in ph.order(g)[c0 // 2:]:
                    pos = ph.pos(g, kind, n)
                    if kind == "ada":
                        ada_load(n, ph.slot(it, pos), ph.landed(it, pos), ph.ada_before(it, g), ph.used(it, pos, 0))
                        continue
                    for c in (2 * n, 2 * n + 1):
                        if c in before:
                            before[c]()
                        lo_chunk(ph, it, g, c)
                        if c in after:
                            after[c]()

            def sums(ph, it, g, dst, half):
                dve.wait_ge(half_ready, ph.group(it, g) + 1)
                nc.vector.tensor_tensor(dst, psum[:, 4 * (g % 2):4 * (g % 2) + GT, 0:SEQ], half[:, :, :],
                                        ALU.add).then_inc(sum_ready, 1)

            def summed(ph, it, g):
                dve.wait_ge(sum_ready, ph.group(it, g) + 1)

            def gain_scale(gain, scale, t0, n):
                link(nc.vector.scalar_tensor_tensor(out=scale_a[:, bass.ds(t0, n)], in0=mod[:, bass.ds(t0 + scale, n)],
                                                    scalar=1.0, in1=par[:, bass.ds(t0 + gain, n)],
                                                    op0=ALU.add, op1=ALU.mult))

            def norm(first, t0, n, shift, buf):
                def lo(i):
                    dve.wait_ge(h_hi, t0 + (first + i + 1))
                    t = bass.ds(t0 + i, 1)
                    nc.vector.scalar_tensor_tensor(out=hT[:, t, SEQ:], in0=buf[:, i % 2:i % 2 + 1, :],
                                                   scalar=mod[:, bass.ds(t0 + (shift + i), 1)],
                                                   in1=hT[:, t, 0:SEQ].bitcast(F32), op0=ALU.add,
                                                   op1=ALU.subtract).then_inc(h_ready, 1)

                for i in range(n):
                    if i >= 2:
                        dve.wait_ge(h_ready, t0 + (first + i - 1))
                    t = bass.ds(t0 + i, 1)
                    nc.vector.scalar_tensor_tensor(out=buf[:, i % 2:i % 2 + 1, :], in0=xT[:, t, :], scalar=scale_a[:, t],
                                                   in1=rs_x[:, :, :], op0=ALU.mult, op1=ALU.mult).then_inc(t_ready, 1)
                    if i >= 1:
                        lo(i - 1)
                lo(n - 1)
                dve.wait_ge(h_ready, t0 + (first + n))

            def accumulate(it, j):
                for q in range(LOAD_T):
                    key = ("pair", it, j, q)
                    ada_load(q, START.slot(*key), START.landed(*key), None, START.used(0, *key), (ada_acc, acc_shift)[j])

            def mixer_store(it, j):
                mod_store(it * 2 + (j + 1), it + (ADA_SC1, ADA_SH1)[j], 1 + j)

            def mixer_norm(it, stored):
                dve.wait_ge(mod_ready, stored)
                gain_scale(PC_GMIX, ADA_SC1 * GT, it * GT, GT)
                norm(0, it * GT, GT, ADA_SH1 * GT, t_x)

            dve.wait_ge(silu_ready, 1)
            accumulate(0, 0)
            accumulate(0, 1)
            dve.wait_ge(rt_ready, 1)
            link(nc.vector.reciprocal(rs_x[:, 0, :], rs_x[:, 0, :]))
            mixer_store(0, 0)
            def first_lo(m):
                for k in range(4 * m, 4 * m + 4):
                    g, half = k % 4 // 2, k % 2
                    dve.wait_ge(hi_ready, k + 1)
                    nc.vector.tensor_tensor(w_lo[:, k % 4, :, :],
                                            raw[:, START.slot("u", m, g), half * CHUNK_T:(half + 1) * CHUNK_T, :],
                                            w_hi[:, k % 4, :, :].bitcast(F32), ALU.subtract).then_inc(half_used, 1)

            def first_sc2(q):
                key = ("sc2", q)
                ada_load(q, START.slot(*key), START.landed(*key), 8, START.used(0, *key), acc_shift)

            def u_rest(g):
                dve.wait_ge(chunk_used, START.chunks_used(g))
                dve.wait_ge(half_ready, g + 1)
                nc.vector.tensor_copy(u_pad[:, g * GT + 2:(g + 1) * GT, PAD:],
                                      bank[5 + 2 * g].rearrange("p (t n) -> p t n", n=SEQ)).then_inc(sum_ready, 1)

            for m in range(1, GT):
                accumulate(m, 0)
                mixer_store(m - 1, 1)
                mixer_norm(m - 1, 2 * m)
                accumulate(m, 1)
                mixer_store(m, 0)
                first_lo(m - 1)
            mixer_store(GT - 1, 1)
            mixer_norm(GT - 1, 2 * GT)
            first_sc2(0)
            first_sc2(1)
            first_lo(GT - 1)
            first_sc2(2)
            first_sc2(3)
            dve.wait_ge(par_ready, 2)
            head(PH_QK, 0, 0, after={1: lambda: u_rest(0), 3: lambda: u_rest(1)})

            def broadcast(a, n):
                return a[:, None, :].to_broadcast([P, n, a.shape[1]])

            def turned(g):
                nc.vector.tensor_tensor(rb[:, :, :], psum[:, 4 * (1 - g):4 * (1 - g) + GT, 0:SEQ],
                                        broadcast(rope_c[:, SEQ:2 * SEQ], GT), ALU.mult).then_inc(rope_sin, 1)

            def turned_q(it):
                dve.wait_ge(d_ready, 1)
                dve.wait_ge(rope_root, it + 1)
                nc.vector.reciprocal(rsq[:, bass.ds(it * (2 * GT), 2 * GT)], root[:, :])
                turned(1)

            with dve.Fori(0, 2) as it:
                step.enter(it, 12)
                for g in range(2):
                    rest(PH_QK, it, g, after={5: lambda: turned_q(it)} if g else ())
                    head(PH_QK, it + g, 1 - g, (it + PH_QK.ada0 + 1, it + (ADA_SC2 + 1), 0) if g else None)
                    sums(PH_QK, it, g, qk[:, bass.ds(it * GT, GT), g, :], half_a)
                dve.wait_ge(rope_out, it + 1)
                step.leave(2)

            def turned_k(g):
                dve.wait_ge(rope_root, 3 + g)
                link(nc.vector.reciprocal(rsk[:, :], root[:, :]))
                nc.vector.tensor_tensor(diag[:, :, :], broadcast(ident, 2 * GT),
                                        rsk[:, :, None].to_broadcast([P, 2 * GT, P]), ALU.mult)
                turned(g)

            def keys(g):
                dve.wait_ge(k_mm, g + 1)
                dve.wait_ge(rope_out, 3 + g)
                k = qk[:, g * GT:(g + 1) * GT, 1, :]
                b0 = 4 * (1 - g)
                scale = psum[:, b0:b0 + 2, :].rearrange("p b n -> p (b n)").rearrange("p (t n) -> p t n", n=SEQ)
                nc.vector.tensor_tensor(k, scale, k, ALU.mult).then_inc(k_ready, 1)

            for g in range(2):
                rest(PH_V, 0, g, after={4: lambda: turned_k(g)})
                head(PH_V if g == 0 else PH_GATE, 0, 1 - g,
                     (PH_V.ada0 + 2, ADA_SC2 + 3, 2) if g else (PH_V.ada0 + 1, ADA_SC2, 6),
                     after={1: lambda: keys(g)})
                dve.wait_ge(half_ready, PH_V.group(0, g) + 1)
                nc.vector.tensor_copy(v_tok[:, 1, g * COLS:(g + 1) * COLS], bank[4 * g + 1][:, :]).then_inc(sum_ready, 1)

            def maxima(it, g):
                dve.wait_ge(s_mm, it * 2 + (g + 1))
                b, pr, st = bank[4 * (1 - g)], probs[:, g, :], stat[:, g, :]
                for n, (lo, hi) in enumerate(((0, P), (P, QW))):
                    ins = nc.vector.scalar_tensor_tensor(out=pr[:, lo:hi], in0=b[:, lo:hi],
                                                         scalar=rsq[:, bass.ds(it * 4 + (2 * g + n), 1)],
                                                         in1=mask[:, lo:hi], op0=ALU.mult, op1=ALU.add)
                link(ins)
                nc.vector.reduce_max(st[:, 0:1], pr[:, 0:P], AX.X)
                link(nc.vector.reduce_max(st[:, 1:2], pr[:, P:QW], AX.X))
                nc.vector.tensor_scalar(st[:, 2:4], st[:, 0:2], -SCALE, None, ALU.mult).then_inc(max_ready, 1)

            def normalise(it, g):
                dve.wait_ge(exp_ready, it * 2 + (g + 1))
                pr, st = probs[:, g, :], stat[:, g, :]
                link(nc.vector.reciprocal(st[:, 6:8], st[:, 4:6]))
                nc.vector.tensor_scalar(pr[:, 0:P], pr[:, 0:P], st[:, 6:7], None, ALU.mult)
                nc.vector.tensor_scalar(pr[:, P:QW], pr[:, P:QW], st[:, 7:8], None, ALU.mult).then_inc(probs_ready, 1)

            def pool_lo(it, g):
                dve.wait_ge(mix_hi, it * 2 + (g + 1))
                o, b = it * 2 + g, 4 * (1 - g) + 3
                nc.vector.scalar_tensor_tensor(out=poolT[:, bass.ds(o, 1), SEQ:], in0=psum[:, b:b + 1, 0:SEQ],
                                               scalar=par[:, bass.ds(o + PC_PSCALE, 1)],
                                               in1=poolT[:, bass.ds(o, 1), 0:SEQ].bitcast(F32), op0=ALU.mult,
                                               op1=ALU.subtract).then_inc(pool_ready, 1)

            def attn_lo(it, g):
                dve.wait_ge(o_hi, it * 2 + (g + 1))
                h, b = it * 2 + g, 4 * (1 - g) + 2
                nc.vector.tensor_tensor(attnT[:, bass.ds(h, 1), SEQ:], psum[:, b:b + 1, 0:SEQ],
                                        attnT[:, bass.ds(h, 1), 0:SEQ].bitcast(F32), ALU.subtract).then_inc(attn_ready, 1)

            with dve.Fori(0, 4) as it:
                step.enter(it, 12 + 2 * 3)
                for g in range(2):
                    rest(PH_GATE, it, g, after={5: lambda: maxima(it, g), 7: lambda: pool_lo(it, g)},
                         before={6: lambda: normalise(it, g)})
                    head(PH_GATE, it + g, 1 - g, (it + (PH_GATE.ada0 + 1), it + ADA_SH2, 0) if g else None,
                         after={2: lambda: attn_lo(it, g)})
                    sums(PH_GATE, it, g, gates[:, bass.ds(it * GT + g * DT, GT), :], half_a)
                step.leave(4)

            def merged_lo(m):
                dve.wait_ge(merge_hi, m + 1)
                t = slice(m * GT, (m + 1) * GT)
                nc.vector.tensor_tensor(hT[:, t, SEQ:], y_sum[:, :, :], hT[:, t, 0:SEQ].bitcast(F32),
                                        ALU.subtract).then_inc(merged_ready, 1)

            dve.wait_ge(gate_ready, 2 * DT)
            for n in range(8):
                it, g = n // 4, n % 4
                rest(PH_BR, it, g)
                lag = {3: lambda: merged_lo(n // 2 - 1)} if n % 2 == 0 and n else ()
                store = (PH_BR.ada0 + it + 1, ADA_G1 + it, 0) if g == 3 else None
                head(PH_BR, it + (g == 3), (g + 1) % 4, store, after=lag)
                if n >= 3 and n % 2:
                    dve.wait_ge(merged_ready, n // 2)
                sums(PH_BR, it, g, (y_attn, y_sum)[g % 2][:, :, :], half_a)
            merged_lo(3)
            dve.wait_ge(merged_ready, 4)
            dve.wait_ge(x_back, 16)
            with dve.Fori(0, 2) as it:
                step.enter(it, 12)
                for g in range(2):
                    rest(PH_WO, it, g)
                    head(PH_WO, it + g, 1 - g, (it + (PH_WO.ada0 + 1), it + (ADA_G1 + 2), 0) if g else None,
                         chunks=3)
                    sums(PH_WO, it, g, y_sum[:, :, :], half_a)
                    summed(PH_WO, it, g)
                    if g:
                        dve.wait_ge(mod_ready, it + (PH_WO.ada0 + 1))
                    for ft in range(GT):
                        t = it * (2 * GT) + (g * GT + ft)
                        ins = nc.vector.scalar_tensor_tensor(
                            out=xT[:, bass.ds(t, 1), :], in0=y_sum[:, ft:ft + 1, :], scalar=mod[:, bass.ds(t + ADA_G1 * GT, 1)],
                            in1=xT[:, bass.ds(t, 1), :], op0=ALU.mult, op1=ALU.add)
                    ins.then_inc(x1_ready, 1)
                    lo_chunk(PH_WO, it + g, 1 - g, 3)
                step.leave(2)
            dve.wait_ge(mod_ready, ADA_G2)
            gain_scale(PC_GFFN, ADA_SC2 * GT, 0, DT)
            dve.wait_ge(rt_ready, 2)
            link(nc.vector.reciprocal(rs_x[:, 0, :], rs_x[:, 0, :]))
            norm(DT, 0, DT, ADA_SH2 * GT, t_x1)

            dve.wait_ge(spilled, 16)
            link(nc.vector.memset(up_pad[:, :, 0:2], 0.0))

            def taps(it, g):
                dst = conv_a if g == 0 else conv_b_

                def tap(ft, j):
                    w = par[:, bass.ds(it * GT + (PC_CONV[j] + g * FT + ft), 1)]
                    return nc.vector.scalar_tensor_tensor(out=dst[:, ft, :], in0=up_pad[:, ft, j:j + SEQ], scalar=w,
                                                          in1=dst[:, ft, :], op0=ALU.mult, op1=ALU.add)

                for ft in range(GT):
                    dve.wait_ge(tap2_ready, it * (2 * GT) + (g * GT + ft + 1))
                    step.inc(tap(ft, 1))
                for ft in range(GT):
                    dve.wait_ge(dve_step, step.value() - (GT - 1 - ft))
                    last = tap(ft, 0)
                last.then_inc(taps_ready, 1)
                dve.wait_ge(taps_ready, it * 2 + (g + 1))

            def glu(it):
                dve.wait_ge(silu_a, it + 1)
                nc.vector.tensor_tensor(conv_b_[:, :, :], conv_b_[:, :, :], conv_a[:, :, :], ALU.mult).then_inc(glu_ready, 1)

            def glu_lo(it):
                dve.wait_ge(act_hi, it + 1)
                t = bass.ds(it * GT, GT)
                nc.vector.tensor_tensor(actT[:, t, SEQ:], conv_b_[:, :, :], actT[:, t, 0:SEQ].bitcast(F32),
                                        ALU.subtract).then_inc(act_ready, 1)
                dve.wait_ge(act_ready, it + 1)

            for c in (4, 5):
                lo_chunk(PH_UP, 0, 0, c)
            with dve.Fori(0, 11) as it:
                step.enter(it, 2 * GT)
                for g in range(2):
                    rest(PH_UP, it, g, c0=4 if g else 6)
                    head(PH_UP, it + g, 1 - g)
                    sums(PH_UP, it, g, up_pad[:, :, 2:], half_b)
                    taps(it, g)
                for c in (4, 5):
                    lo_chunk(PH_UP, it + 1, 0, c)
                glu(it)
                glu_lo(it)
                step.leave(11)

            def copy_out(n, G, b):
                dve.wait_ge(out_mm, n + 1)
                nc.vector.tensor_copy(out_tok[:, G, 1, :], bank[b + 1][:, :]).then_inc(out_copied[1], 1)

            for it in range(2):
                for g in range(2):
                    G = 2 * it + g
                    rest(PH_DOWN, it, g, after={9: lambda: copy_out(it, 2 * it, 0)} if g else (), c0=4 if G else 6)
                    store = (PH_DOWN.ada0 + G + 1, ADA_G2 + G, 4 * (1 - g))
                    if G < 3:
                        head(PH_DOWN, it + g, 1 - g, store)
                    else:
                        mod_store(*store)
                    sums(PH_DOWN, it, g, conv_a[:, :, :], half_b)
                    summed(PH_DOWN, it, g)
                    dve.wait_ge(mod_ready, PH_DOWN.ada0 + G + 1)
                    dve.wait_ge(x1_back, 16)
                    for ft in range(GT):
                        t = G * GT + ft
                        dst = x2T[:, t, :] if g else x2_even[:, ft, :]
                        nc.vector.scalar_tensor_tensor(
                            out=dst, in0=conv_a[:, ft, :], scalar=mod[:, ADA_G2 * GT + t:ADA_G2 * GT + t + 1],
                            in1=x2T[:, t, :], op0=ALU.mult, op1=ALU.add).then_inc(x2_ready, 1)
                    dve.wait_ge(x2_ready, (G + 1) * GT)
            for n, G, b in ((2, 1, 2), (3, 3, 0)):
                copy_out(n, G, b)

        @block.tensor
        def _(pe):
            def main_chunk(ph, it, g, c, x, value=False):
                n_chunks, sc = ph.chunks, ph.chunk_slot(g, c)
                pos = ph.pos(g, "main", c * CHUNK_T // LOAD_T)
                pe.wait_ge(half_used, ph.used(it, pos, c % 2 + 1))
                for t in range(CHUNK_T):
                    k = c * CHUNK_T + t
                    first, final = k == 0, k == n_chunks * CHUNK_T - 1
                    if value:
                        for tok in range(2):
                            b = bank[4 * (g % 2) + tok]
                            hi, lo = (x[:, k, o + tok * P:o + (tok + 1) * P] for o in (0, SEQ))
                            nc.tensor.matmul(b[:, :], hi, w_hi[:, sc, t, :], start=first, stop=False)
                            nc.tensor.matmul(b[:, :], hi, w_lo[:, sc, t, :], start=False, stop=False)
                            last = nc.tensor.matmul(b[:, :], lo, w_hi[:, sc, t, :], start=False, stop=final)
                        continue
                    for ft in range(GT):
                        b = bank[4 * (g % 2) + ft]
                        hi, lo = (w[:, sc, t, ft * P:(ft + 1) * P] for w in (w_hi, w_lo))
                        if t == 0:
                            nc.tensor.matmul(b[:, :], hi, x[:, k, :], start=first, stop=False)
                            last = nc.tensor.matmul(b[:, 0:SEQ], lo, x[:, k, 0:SEQ], start=False, stop=False)
                        else:
                            nc.tensor.matmul(b[:, 0:SEQ], lo, x[:, k, 0:SEQ], start=False, stop=False)
                            last = nc.tensor.matmul(b[:, :], hi, x[:, k, :], start=False, stop=final)
                last.then_inc(chunk_used, 1)

            def ada_reduce(b, acc=ada_acc):
                for ft in range(GT):
                    for n in range(2):
                        last = nc.tensor.matmul(bank[b][:, ft:ft + 1], acc[:, n, ft * P:(ft + 1) * P], ones[:, 0:1],
                                                start=n == 0, stop=n == 1)
                last.then_inc(ada_sum, 1)

            def group(ph, it, g, x, value=False, ready=None, between=(), ada_bank=0, held=None):
                pe.wait_ge(sum_ready, ph.group(it, g - 1))
                pe.wait_ge(mod_ready, ph.ada_before(it, g))
                n_chunks = ph.chunks
                for c in range(n_chunks):
                    if ready:
                        ready(c)
                    if c in between:
                        pe.wait_ge(sum_ready, ph.group(it, g))
                        between[c]()
                    if c == n_chunks - 1 and ph.reduces(g):
                        if held is None:
                            pe.wait_ge(half_used, ph.used(it, ph.pos(g, "ada", 3), 2))
                        pe.wait_ge(sum_ready, ph.group(it, g))
                        ada_reduce(4 * (1 - g % 2) + ada_bank, ada_acc if held is None else held)
                    main_chunk(ph, it, g, c, x, value)

            pe.wait_ge(square_in, 16)
            pe.wait_ge(par_in, 3 * 16)
            nc.tensor.transpose(bank[7][:, 0:P], par_rows[:, 0, :], ident).then_inc(par_mm, 1)
            pe.wait_ge(x_in, 16)
            for b in range(8):
                if b == 7:
                    pe.wait_ge(par_ready, 1)
                for n in range(4):
                    t, tok = 2 * b + n // 2, n % 2
                    last = nc.tensor.transpose(bank[b][:, n * P:(n + 1) * P], x_tok[:, tok, t * P:(t + 1) * P], ident)
                last.then_inc(xt_mm, 1)
            for b in range(8):
                pe.wait_ge(sqx_ready, b + 1)
                for n in range(2):
                    last = nc.tensor.matmul(bank[0][:, 0:SEQ], ones, sq_x[:, b % 2, n * SEQ:(n + 1) * SEQ],
                                            start=b + n == 0, stop=b + n == 8)
                last.then_inc(sqx_used, 1)
            pe.wait_ge(par_in2, 9 * 16)
            for n in range(1, 6):
                r = PBLOCK_ROWS[n]
                b, o = (bank[5], (n - 1) * P) if n < 5 else (bank[6], 0)
                last = nc.tensor.transpose(b[:, o:o + r], par_rows[0:r, n, :], ident[0:r, 0:r])
            last.then_inc(par_mm, 1)

            def mixer_sums(it):
                for j, acc in enumerate((ada_acc, acc_shift)):
                    pe.wait_ge(half_used, START.used(2, "pair", it, j, LOAD_T - 1))
                    if it:
                        pe.wait_ge(mod_ready, it * 2 + (j - 1))
                    ada_reduce(1 + j, acc)

            def first_products(m):
                for k in range(4 * m, 4 * m + 4):
                    g, half = k % 4 // 2, k % 2
                    pe.wait_ge(half_used, START.used(half + 1, "u", m, g))
                    for t in range(CHUNK_T):
                        n = m * LOAD_T + half * CHUNK_T + t
                        pe.wait_ge(h_ready, n + 1)
                        for ft in range(GT):
                            o = bank[4 + 2 * g + ft // 2][:, (ft % 2) * SEQ:(ft % 2 + 1) * SEQ]
                            hi, lo = (w[:, k % 4, t, ft * P:(ft + 1) * P] for w in (w_hi, w_lo))
                            nc.tensor.matmul(o, hi, hT[:, n, 0:SEQ], start=n + ft % 2 == 0, stop=False)
                            nc.tensor.matmul(o, hi, hT[:, n, SEQ:], start=False, stop=False)
                            last = nc.tensor.matmul(o, lo, hT[:, n, 0:SEQ], start=False, stop=n == DT - 1 and ft % 2 == 1)
                    last.then_inc(chunk_used, 1)

            mixer_sums(0)
            mixer_sums(1)
            pe.wait_ge(par_ready, 2)
            for m in range(GT):
                first_products(m)
                if m < GT - 2:
                    mixer_sums(m + 2)

            def turn(r, g):
                pe.wait_ge(rope_in, r + 1)
                b0 = 4 * (1 - g)
                for ft in range(GT):
                    nc.tensor.matmul(bank[b0 + ft][:, 0:SEQ], rope_c[:, 2 * SEQ:], tg[:, ft, :], start=True, stop=True)
                for ft in range(GT):
                    for tok in range(2):
                        n = SEQ + 2 * ft + tok
                        last = nc.tensor.matmul(bank[b0][:, n:n + 1], sq[:, ft, tok * P:(tok + 1) * P], ones[:, 0:1],
                                                start=True, stop=True)
                last.then_inc(rope_mm, 1)

            def key_scale(r, g):
                pe.wait_ge(rope_sin, r + 1)
                b0 = 4 * (1 - g)
                for n in range(2):
                    last = nc.tensor.matmul(bank[b0 + n][:, :], ones, diag[:, n * GT:(n + 1) * GT, :], start=True, stop=True)
                last.then_inc(k_mm, 1)

            pe.wait_ge(const_in, 48)
            with pe.Fori(0, 2) as it:
                group(PH_QK, it, 0, hT)
                group(PH_QK, it, 1, hT, between={4: lambda: turn(it, 1)})
                pe.wait_ge(rope_sin, it + 1)
            for g in range(2):
                group(PH_V, 0, g, hT, value=True, ada_bank=2, held=None if g else acc_shift,
                      between={2: lambda: turn(2 + g, g), 5: lambda: key_scale(2 + g, g)})
                pe.wait_ge(k_ready, g + 1)

            def scores(it, g):
                pe.wait_ge(stage_ready, it * 2 + (g + 1))
                b = bank[4 * (1 - g)]
                k = qk[:, bass.ds(it * 2 + g, 1), 1, :].rearrange("p a n -> p (a n)")
                nc.tensor.matmul(b[:, 0:P], q_st[:, g, 0:P], k[:, 0:P], start=True, stop=True)
                nc.tensor.matmul(b[:, P:QW], q_st[:, g, P:SEQ], k, start=True, stop=True).then_inc(s_mm, 1)

            def turn_probs(it, g):
                pe.wait_ge(probs_ready, it * 2 + (g + 1))
                for n in range(3):
                    last = nc.tensor.transpose(bank[4 * (1 - g) + 1][:, n * P:(n + 1) * P],
                                               probs[:, g, n * P:(n + 1) * P], ident)
                last.then_inc(pt_mm, 1)

            def output(it, g):
                pe.wait_ge(pt_ready, it * 2 + (g + 1))
                b = bank[4 * (1 - g) + 2]
                nc.tensor.matmul(b[:, 0:SEQ], v_st[:, g, 0, :], probsT[:, g, 0:SEQ], start=True, stop=False)
                nc.tensor.matmul(b[:, P:SEQ], v_st[:, g, 1, :], probsT[:, g, SEQ:QW], start=False,
                                 stop=True).then_inc(o_mm, 1)

            def mix(it, g):
                pe.wait_ge(wp_in[g], it * 16 + 16)
                for t in range(2):
                    u = u_pad[:, bass.ds(it * 2 + t, 1), PAD:].rearrange("p a n -> p (a n)")
                    last = nc.tensor.matmul(bank[4 * (1 - g) + 3][:, 0:SEQ], wp_st[:, g, t, :], u,
                                            start=t == 0, stop=t == 1)
                last.then_inc(mix_mm, 1)

            pe.wait_ge(d_ready, 1)
            with pe.Fori(0, 4) as it:
                for g in range(2):
                    group(PH_GATE, it, g, hT, between={2: lambda: scores(it, g), 4: lambda: mix(it, g),
                                                      6: lambda: turn_probs(it, g), 7: lambda: output(it, g)})
                    pe.wait_ge(pool_ready, it * 2 + (g + 1))
                    pe.wait_ge(attn_ready, it * 2 + (g + 1))
            with pe.Fori(0, 2) as it:
                for g in range(4):
                    group(PH_BR, it, g, poolT if g % 2 else attnT)
            with pe.Fori(0, 2) as it:
                group(PH_WO, it, 0, hT,
                      ready=lambda c: pe.wait_ge(merged_ready, 3 if c < 6 else 4) if c in (0, 6) else None)
                group(PH_WO, it, 1, hT)
            pe.wait_ge(ss_ready, 4)
            pe.wait_ge(mod_ready, PH_WO.ada_end)
            for n, squares in enumerate((ss_x1, sq_x1)):
                if n:
                    pe.wait_ge(sq1_ready, 4)
                for ft in range(GT):
                    last = nc.tensor.matmul(bank[0][:, 0:SEQ], ones, squares[:, ft, :], start=n + ft == 0,
                                            stop=n + ft == GT)
            last.then_inc(ss_mm, 1)

            def result(tiles, b0):
                for tok in range(2):
                    for ft in range(GT):
                        last = nc.tensor.transpose(bank[b0 + tok][:, ft * P:(ft + 1) * P],
                                                   tiles[:, ft, tok * P:(tok + 1) * P], ident)
                last.then_inc(out_mm, 1)

            def even_result(it):
                pe.wait_ge(x2_ready, it * (2 * GT) + GT)
                result(x2_even, 0)

            with pe.Fori(0, 11) as it:
                group(PH_UP, it, 0, hT, ready=lambda c: pe.wait_ge(h_ready, DT + (c + 1) * CHUNK_T))
                group(PH_UP, it, 1, hT)
            with pe.Fori(0, 2) as it:
                group(PH_DOWN, it, 0, actT,
                      ready=lambda c: pe.wait_ge(act_ready, 10 if c < 20 else 11) if c in (0, 20) else None)
                group(PH_DOWN, it, 1, actT, between={8: lambda: even_result(it)})
                for n in range(2):
                    pe.wait_ge(out_copied[n], it + 1)
            result(x2T[:, GT:2 * GT, :], 2)
            pe.wait_ge(x2_ready, 4 * GT)
            result(x2T[:, 3 * GT:, :], 0)


_INS = ["x", "c", "w_ada", "b_ada", "norm_mix_g", "w_in", "q_norm_g", "k_norm_g", "w_pool_grp", "pool_scale",
        "w_attn_br", "w_pool_br", "w_gate", "b_gate", "w_o", "norm_ffn_g", "w_up", "conv_w", "conv_b", "w_down"]


def shape_constants():
    square = np.stack([np.eye(P, dtype=np.float32), np.ones((P, P), np.float32)], 1)
    half = HD // 2
    inv = np.float32(10000.0) ** (-np.arange(half, dtype=np.float32) / np.float32(half))
    ang = (np.arange(SEQ, dtype=np.float32)[None, :] * inv.astype(np.float32)[:, None]).astype(np.float32)
    turn = np.zeros((P, P), np.float32)
    turn[np.arange(half) + half, np.arange(half)] = -1.0
    turn[np.arange(half), np.arange(half) + half] = 1.0
    rope = np.concatenate([np.tile(np.cos(ang), (2, 1)), np.tile(np.sin(ang), (2, 1)), turn], 1).astype(np.float32)
    later = np.where(np.arange(P)[None, :] > np.arange(P)[:, None], np.float32(NEG), np.float32(0))
    mask = np.concatenate([later, np.zeros((P, P), np.float32), later], 1).astype(np.float32)
    counts = np.stack([np.minimum(np.arange(SEQ) + 1, w) for w in POOL_WINDOWS])
    invcnt = np.broadcast_to((1.0 / counts).astype(np.float32), (P, 4, SEQ)).copy()
    return {"k_square": square, "k_rope": rope, "k_mask": mask, "k_invcnt": invcnt}


def kernel(**inputs):
    import concourse.bacc as _bacc
    from concourse.bass_utils import run_bass_kernel_spmd as _run

    nc = _bacc.Bacc("TRN2", target_bir_lowering=False, num_devices=1)
    arrays, args = {}, []
    given = {name: np.ascontiguousarray(inputs[name]) for name in _INS}
    given.update(shape_constants())
    for name, a in given.items():
        arrays[f"in_{name}"] = a
        args.append(nc.dram_tensor(f"in_{name}", a.shape, mybir.dt.from_np(a.dtype), kind="ExternalInput").ap())
    args.append(nc.dram_tensor("out", (1, SEQ, D), F32, kind="ExternalOutput").ap())
    args.append(nc.dram_tensor("x1_spill", (P, DT * SEQ), F32, kind="Internal").ap())
    build_block(nc, *args)
    r = _run(nc, [arrays], core_ids=[0])
    return r.results[0]["out"]
```
